# Optimizing a Trainium2 kernel written in Bass

```python
import jax, jax.numpy as jnp
from jax import lax
import numpy as np

D_MODEL = 1024
BATCH = 1
SEQ = 256
DEPTH = 2

N_EVEN = (DEPTH + 1) // 2
N_ODD = DEPTH // 2
RMS_EPS = 1e-5
LN_EPS = 1e-5

D_CONV = D_MODEL // 2
D_POOL = D_MODEL // 2
CONV_K = 31
POOL_WINDOWS = (2, 4, 8, 16)
N_POOL_GROUPS = len(POOL_WINDOWS)
POOL_GROUP = D_POOL // N_POOL_GROUPS
D_IN_EVEN = 2 * D_CONV + D_POOL
D_FF_DENSE = ((8 * D_MODEL // 3 + 127) // 128) * 128

HEAD_DIM = 64
N_Q_HEADS = D_MODEL // HEAD_DIM
N_KV_HEADS = 4
GQA_GROUP = N_Q_HEADS // N_KV_HEADS
WINDOW = 128
ATTN_BLOCK = 128
D_QKV = (N_Q_HEADS + 2 * N_KV_HEADS) * HEAD_DIM

N_EXPERTS = 8
TOP_K = 2
D_FF_EXPERT = 7 * D_MODEL // 2

kernel_name = "hybrid_conv_pool_swa_moe_trunk"

def rmsnorm(x, g):
    xf = x.astype(jnp.float32)
    y = xf * lax.rsqrt(jnp.mean(xf * xf, axis=-1, keepdims=True) + RMS_EPS)
    return (y * g.astype(jnp.float32)).astype(x.dtype)

def layernorm(x, g, b):
    xf = x.astype(jnp.float32)
    mu = jnp.mean(xf, axis=-1, keepdims=True)
    var = jnp.mean(jnp.square(xf - mu), axis=-1, keepdims=True)
    y = (xf - mu) * lax.rsqrt(var + LN_EPS)
    return (y * g.astype(jnp.float32) + b.astype(jnp.float32)).astype(x.dtype)

def swiglu(t, w1, w3, w2):
    return (jax.nn.silu(t @ w1) * (t @ w3)) @ w2

def causal_depthwise_conv(u, w, b):
    up = jnp.pad(u, ((0, 0), (CONV_K - 1, 0), (0, 0)))
    y = lax.conv_general_dilated(
        up, w.astype(u.dtype)[:, None, :], window_strides=(1,), padding='VALID',
        dimension_numbers=('NWC', 'WIO', 'NWC'), feature_group_count=u.shape[-1])
    return y + b.astype(u.dtype)

def multiscale_causal_pool(u):
    bsz, s, _ = u.shape
    ug = u.reshape(bsz, s, N_POOL_GROUPS, POOL_GROUP).astype(jnp.float32)
    cs = jnp.cumsum(ug, axis=1)
    pos = jnp.arange(s)
    pooled = []
    for g, w in enumerate(POOL_WINDOWS):
        c = cs[:, :, g]
        lag = jnp.pad(c, ((0, 0), (w, 0), (0, 0)))[:, :s]
        cnt = jnp.minimum(pos + 1, w).astype(jnp.float32)[None, :, None]
        pooled.append((c - lag) / cnt)
    pooled = jnp.stack(pooled, axis=2)
    return (pooled - ug).astype(u.dtype)

def conv_pool_mixer(hn, w_in, conv_w, conv_b, ln_g, ln_b, pool_w, pool_scale, w_out):
    bsz, s, _ = hn.shape
    u = hn @ w_in
    a_val = u[..., :D_CONV]
    a_gate = u[..., D_CONV:2 * D_CONV]
    b_in = u[..., 2 * D_CONV:]
    a = a_val * jax.nn.sigmoid(a_gate)
    a = causal_depthwise_conv(a, conv_w, conv_b)
    a = jax.nn.silu(layernorm(a, ln_g, ln_b))
    p = multiscale_causal_pool(b_in)
    p = jnp.einsum('bsgc,gcd->bsgd', p, pool_w).reshape(bsz, s, D_POOL)
    p = p * pool_scale
    return jnp.concatenate([a, p], axis=-1) @ w_out

def sliding_window_sink_attention(q, k, v, sinks):
    bsz, s = q.shape[:2]
    nb = s // ATTN_BLOCK
    qb = q.reshape(bsz, nb, ATTN_BLOCK, N_KV_HEADS, GQA_GROUP, HEAD_DIM)

    def with_prev_block(t):
        tb = t.reshape(bsz, nb, ATTN_BLOCK, N_KV_HEADS, HEAD_DIM)
        prev = jnp.pad(tb, ((0, 0), (1, 0), (0, 0), (0, 0), (0, 0)))[:, :-1]
        return jnp.concatenate([prev, tb], axis=2)

    kc = with_prev_block(k)
    vc = with_prev_block(v)
    scores = jnp.einsum('bnqkgd,bnskd->bnkgqs', qb, kc).astype(jnp.float32)
    scores = scores * (HEAD_DIM ** -0.5)
    blk = jnp.arange(nb)[:, None, None]
    qpos = blk * ATTN_BLOCK + jnp.arange(ATTN_BLOCK)[None, :, None]
    kpos = (blk - 1) * ATTN_BLOCK + jnp.arange(2 * ATTN_BLOCK)[None, None, :]
    diff = qpos - kpos
    mask = (diff >= 0) & (diff < WINDOW) & (kpos >= 0)
    scores = jnp.where(mask[None, :, None, None], scores, -jnp.inf)
    sink = sinks.astype(jnp.float32).reshape(N_KV_HEADS, GQA_GROUP)[None, None, :, :, None, None]
    m = jnp.maximum(jnp.max(scores, axis=-1, keepdims=True), sink)
    e = jnp.exp(scores - m)
    denom = jnp.sum(e, axis=-1, keepdims=True) + jnp.exp(sink - m)
    probs = (e / denom).astype(v.dtype)
    out = jnp.einsum('bnkgqs,bnskd->bnqkgd', probs, vc)
    return out.reshape(bsz, s, N_Q_HEADS * HEAD_DIM)

def swa_mixer(hn, w_qkv, b_qkv, sinks, w_o, b_o):
    bsz, s, _ = hn.shape
    u = hn @ w_qkv + b_qkv
    dq = N_Q_HEADS * HEAD_DIM
    dk = N_KV_HEADS * HEAD_DIM
    q = u[..., :dq].reshape(bsz, s, N_Q_HEADS, HEAD_DIM)
    k = u[..., dq:dq + dk].reshape(bsz, s, N_KV_HEADS, HEAD_DIM)
    v = u[..., dq + dk:].reshape(bsz, s, N_KV_HEADS, HEAD_DIM)
    o = sliding_window_sink_attention(q, k, v, sinks)
    return o @ w_o + b_o

def moe_swiglu(hn, router_w, w1, w3, w2):
    bsz, s, d = hn.shape
    t = hn.reshape(-1, d)
    logits = (t @ router_w).astype(jnp.float32)
    top_v, top_i = lax.top_k(logits, TOP_K)
    gates = jax.nn.softmax(top_v, axis=-1)
    gate_te = jnp.sum(jax.nn.one_hot(top_i, N_EXPERTS, dtype=jnp.float32) * gates[..., None], axis=1)
    gate_te = gate_te.astype(t.dtype)
    out = jnp.zeros_like(t)
    for e in range(N_EXPERTS):
        out = out + gate_te[:, e:e + 1] * swiglu(t, w1[e], w3[e], w2[e])
    return out.reshape(bsz, s, d)

def _normal(k, shape, scale):
    return jax.random.normal(k, shape, jnp.float32) * scale

def setup_inputs(seed: int = 0) -> dict:
    key = jax.random.key(seed)
    ks = jax.random.split(key, 27)
    D = D_MODEL
    return {
        "x": _normal(ks[0], (BATCH, SEQ, D), 1.0),
        "e_norm1": 1.0 + _normal(ks[1], (N_EVEN, D), 0.05),
        "e_w_in": _normal(ks[2], (N_EVEN, D, D_IN_EVEN), D ** -0.5),
        "e_conv_w": _normal(ks[3], (N_EVEN, CONV_K, D_CONV), CONV_K ** -0.5),
        "e_conv_b": _normal(ks[4], (N_EVEN, D_CONV), 0.02),
        "e_ln_g": 1.0 + _normal(ks[5], (N_EVEN, D_CONV), 0.05),
        "e_ln_b": _normal(ks[6], (N_EVEN, D_CONV), 0.02),
        "e_pool_w": _normal(ks[7], (N_EVEN, N_POOL_GROUPS, POOL_GROUP, POOL_GROUP), POOL_GROUP ** -0.5),
        "e_pool_scale": 1.0 + _normal(ks[8], (N_EVEN, D_POOL), 0.05),
        "e_w_out": _normal(ks[9], (N_EVEN, D, D), D ** -0.5),
        "e_norm2": 1.0 + _normal(ks[10], (N_EVEN, D), 0.05),
        "e_ff_w1": _normal(ks[11], (N_EVEN, D, D_FF_DENSE), D ** -0.5),
        "e_ff_w3": _normal(ks[12], (N_EVEN, D, D_FF_DENSE), D ** -0.5),
        "e_ff_w2": _normal(ks[13], (N_EVEN, D_FF_DENSE, D), D_FF_DENSE ** -0.5),
        "o_norm1": 1.0 + _normal(ks[14], (N_ODD, D), 0.05),
        "o_w_qkv": _normal(ks[15], (N_ODD, D, D_QKV), D ** -0.5),
        "o_b_qkv": _normal(ks[16], (N_ODD, D_QKV), 0.02),
        "o_sinks": _normal(ks[17], (N_ODD, N_Q_HEADS), 0.5),
        "o_w_o": _normal(ks[18], (N_ODD, N_Q_HEADS * HEAD_DIM, D), (N_Q_HEADS * HEAD_DIM) ** -0.5),
        "o_b_o": _normal(ks[19], (N_ODD, D), 0.02),
        "o_norm2": 1.0 + _normal(ks[20], (N_ODD, D), 0.05),
        "o_router": _normal(ks[21], (N_ODD, D, N_EXPERTS), D ** -0.5),
        "o_exp_w1": _normal(ks[22], (N_ODD, N_EXPERTS, D, D_FF_EXPERT), D ** -0.5),
        "o_exp_w3": _normal(ks[23], (N_ODD, N_EXPERTS, D, D_FF_EXPERT), D ** -0.5),
        "o_exp_w2": _normal(ks[24], (N_ODD, N_EXPERTS, D_FF_EXPERT, D), D_FF_EXPERT ** -0.5),
        "final_norm": 1.0 + _normal(ks[25], (D,), 0.05),
    }

def reference(x, e_norm1, e_w_in, e_conv_w, e_conv_b, e_ln_g, e_ln_b, e_pool_w, e_pool_scale,
              e_w_out, e_norm2, e_ff_w1, e_ff_w3, e_ff_w2, o_norm1, o_w_qkv, o_b_qkv, o_sinks,
              o_w_o, o_b_o, o_norm2, o_router, o_exp_w1, o_exp_w3, o_exp_w2, final_norm):
    h = x
    for layer in range(DEPTH):
        i = layer // 2
        if layer % 2 == 0:
            h = h + conv_pool_mixer(rmsnorm(h, e_norm1[i]), e_w_in[i], e_conv_w[i], e_conv_b[i],
                                    e_ln_g[i], e_ln_b[i], e_pool_w[i], e_pool_scale[i], e_w_out[i])
            h = h + swiglu(rmsnorm(h, e_norm2[i]), e_ff_w1[i], e_ff_w3[i], e_ff_w2[i])
        else:
            h = h + swa_mixer(rmsnorm(h, o_norm1[i]), o_w_qkv[i], o_b_qkv[i], o_sinks[i],
                              o_w_o[i], o_b_o[i])
            h = h + moe_swiglu(rmsnorm(h, o_norm2[i]), o_router[i], o_exp_w1[i], o_exp_w3[i],
                               o_exp_w2[i])
    return rmsnorm(h, final_norm)


_drawn_inputs = setup_inputs


def setup_inputs(seed=0):
    import zlib

    import numpy as np

    out = dict(_drawn_inputs(seed))
    spreads = {}
    factors = {'o_sinks': 4.632, 'e_ln_b': 2.698, 'o_norm1': 2.955, 'o_b_o': 5.51}
    for name, (base, spread) in spreads.items():
        noise = np.random.default_rng([zlib.crc32(name.encode()), seed]).standard_normal(out[name].shape)
        drawn = base * np.exp(spread * noise) if base else spread * noise
        out[name] = __import__('jax').numpy.asarray(drawn.astype(out[name].dtype))
    for name, factor in factors.items():
        out[name] = (out[name] * factor).astype(out[name].dtype)
    return out
```

```python
from contextlib import ExitStack

import concourse.bass as bass
from concourse import mybir

F32 = mybir.dt.float32
I32 = mybir.dt.int32
ALU = mybir.AluOpType
ACT = mybir.ActivationFunctionType
X = mybir.AxisListType.X

P = 128
KIB = 1024


def hybrid_trunk(nc, x, e_norm1, e_w_in, e_conv_w, e_conv_b, e_ln_g, e_ln_b, e_pool_w, e_pool_scale,
                 e_w_out, e_norm2, e_ff_w1, e_ff_w3, e_ff_w2, o_norm1, o_w_qkv, o_b_qkv, o_sinks,
                 o_w_o, o_b_o, o_norm2, o_router, o_exp_w1, o_exp_w3, o_exp_w2, final_norm, out):
    SEQ, D = x.shape[1], x.shape[2]
    NB = SEQ // P
    KD = D // P
    CONV_K, D_CONV = e_conv_w.shape[1], e_conv_w.shape[2]
    KC = D_CONV // P
    NG = e_pool_w.shape[1]
    D_IN = e_w_in.shape[2]
    FF = e_ff_w1.shape[2] // P
    NH = o_sinks.shape[1]
    NKV = 4
    HD = D // NH
    D_QKV = o_w_qkv.shape[2]
    NE = o_router.shape[2]
    FE = o_exp_w1.shape[3] // P
    RMS_EPS = LN_EPS = 1e-5
    SCALE = HD ** -0.5
    NEG = -1e30
    assert NB == 2 and KD == 8 and HD == 64 and NG == 4 and KC == 4

    JOB = P
    MAX_JOBS = NE + (2 * SEQ) // (JOB + 1)
    NJ = MAX_JOBS + 1
    HALF = FE // 2
    UPS, DOWNS = HALF // 2, HALF // 2

    UP_BYTES = 2 * KD * 2 * P * 4
    DOWN_BYTES = D * 4
    W_BYTES = UPS * UP_BYTES + DOWNS * DOWN_BYTES
    FF_UNITS = FF // 2
    FF_BYTES = 3 * KD * P * 4
    FF_AT = W_BYTES - FF_UNITS * FF_BYTES
    QKV_AT = 80 * KIB
    W_OUT_AT = KD * D_IN * 4
    W_O_AT = 0
    up_slot = [(g + 2) % UPS for g in range(UPS)]
    down_slot = [(i + 4) % DOWNS for i in range(DOWNS)]
    ff_unit = [(j + 6) % FF_UNITS for j in range(FF_UNITS)]

    with ExitStack() as ctx:
        def sb(name, shape, dt=F32):
            return ctx.enter_context(nc.sbuf_tensor(name, shape, dt))

        def sem(name):
            return ctx.enter_context(nc.semaphore(name))

        W = sb("weights", [P, W_BYTES // 4])

        def w_at(at, *dims):
            n = 1
            for d in dims:
                n *= d
            names = "abcd"[:len(dims)]
            return W[:, at // 4:at // 4 + n].rearrange(
                f"p ({' '.join(names)}) -> p {' '.join(names)}", **{c: d for c, d in zip(names, dims)})

        w_in = w_at(0, KD, D_IN)
        w_out = w_at(W_OUT_AT, KD, D)
        w_qkv = w_at(QKV_AT, KD, D_QKV)
        w_o = w_at(W_O_AT, KD, D)
        ff_up = [w_at(FF_AT + u * FF_BYTES, 2, KD, P) for u in range(FF_UNITS)]
        ff_down = [w_at(FF_AT + u * FF_BYTES + 2 * KD * P * 4, D) for u in range(FF_UNITS)]
        exp_up = [w_at(s * UP_BYTES, 2, KD, 2 * P) for s in range(UPS)]
        exp_down = [w_at(UPS * UP_BYTES + s * DOWN_BYTES, D) for s in range(DOWNS)]

        PS = ctx.enter_context(nc.psum_tensor("banks", [P, 8, 512], F32))

        hT = sb("residual_T", [P, KD, SEQ])
        hn = sb("normed_T", [P, KD, SEQ])
        sq = sb("squares", [P, KD, SEQ])
        nat = sb("natural", [P, NB, D])
        area = sb("area", [P, 7168])
        ident = sb("ident", [P, P])
        ones = sb("ones", [P, P])
        tri = sb("tri", [P, P])
        iota_f = sb("iota_f", [P, P])
        vec_rows, conv_rows = hn[0:68, 0, 0:P], hn[0:CONV_K, 1:3, :].rearrange("p k n -> p (k n)")
        iota_i = hn[:, 3, 0:P].bitcast(I32)
        vec = sb("vec", [P, 68])
        conv_w = sb("conv_w", [P, KC, CONV_K])
        inv_cnt = sb("inv_cnt", [P, NG, 16])
        std = sb("std", [P, SEQ])
        rstd = sb("rstd", [P, SEQ])
        sinks = sb("sinks", [P, NH])
        router = sb("router", [P, KD, NE])
        small = sb("small", [P, 352])
        jobs_i = sb("jobs_i", [1, 3, NJ], I32)
        eps = sb("eps", [P, 1])

        taken = [0]

        def part(*dims, reset=False):
            if reset:
                taken[0] = 0
            n = 1
            for d in dims:
                n *= d
            at = taken[0]
            taken[0] += n
            assert taken[0] <= 7168
            names = "abcd"[:len(dims)]
            return area[:, at:at + n].rearrange(
                f"p ({' '.join(names)}) -> p {' '.join(names)}", **{c: d for c, d in zip(names, dims)})

        PADC, PADP = CONV_K - 1, 16
        glu = part(KC, PADC + SEQ, reset=True)
        conv = part(KC, SEQ)
        conv_b2 = part(SEQ)
        mix = part(KD, SEQ)
        pool_in = part(NG, PADP + SEQ)
        pool_t = part(2, PADP + SEQ)
        sig = part(2, SEQ)
        pool_w = part(NG, P)
        ff_sg = part(2, SEQ, reset=True)
        ff_h = part(2, SEQ)
        kT = part(NKV, SEQ, reset=True)
        vN = part(NB, NKV * HD)
        mask = part(3 * P)
        probs = sq[:, 0:6, :].rearrange("p k n -> p (k n)").rearrange("p (h n) -> p h n", h=4)
        b_v = part(NKV * HD)[0:1, :]
        probsT = part(4, 3 * P)
        oT = part(KD, SEQ)
        q = nat[:, :, :].rearrange("p b (k n) -> p (b k) n", n=SEQ)
        mx = small[:, 0:2 * NH]
        negm = small[:, 32:32 + 2 * NH]
        rsum = small[:, 64:64 + 2 * NH]
        esink = small[:, 96:96 + 2 * NH]
        den = small[:, 128:128 + 2 * NH]
        rden = small[:, 160:160 + 2 * NH]
        ys = part(D, reset=True)
        sel = part(NB, P)
        selT = part(NB * P)
        exp_sg = part(2, P)
        exp_h = part(2, P)
        fnorm = part(D)
        res = part(NB, D)
        logits = small[:, 192:208].rearrange("p (b e) -> p b e", b=NB)
        less = small[:, 208:224].rearrange("p (b e) -> p b e", b=NB)
        place = small[:, 224:240].rearrange("p (b e) -> p b e", b=NB)
        first = small[:, 240:256].rearrange("p (b e) -> p b e", b=NB)
        second = small[:, 256:272].rearrange("p (b e) -> p b e", b=NB)
        chosen = small[:, 272:288].rearrange("p (b e) -> p b e", b=NB)
        gates = small[:, 288:304].rearrange("p (b e) -> p b e", b=NB)
        slots = small[:, 304:320].rearrange("p (b e) -> p b e", b=NB)
        iota_e = small[:, 320:336].rearrange("p (b e) -> p b e", b=NB)
        top1, top2, arg = small[:, 336:338], small[:, 338:340], small[:, 340:342]
        ratio, share1, share2 = small[:, 342:344], small[:, 344:346], small[:, 346:348]
        ssq = small[:, 348:350]
        frstd = small[:, 350:352]
        jt = part(4, NJ, NE)
        je = sb("job_rows", [P, 8, 16])
        xg = hT[:, :, :].rearrange("p k n -> p (k n)")[:, 0:KD * P].rearrange("p (k n) -> p k n", n=P)
        yT = hn[:, :, :].rearrange("p k n -> p (k n)")[:, 0:KD * P].rearrange("p (k n) -> p k n", n=P)
        tN = sq[:, :, :].rearrange("p k n -> p (k n)").rearrange("p (b d) -> p b d", b=NB)

        VEC = {}
        at = 0
        for name, ap, n in (("norm1", e_norm1, 8), ("conv_b", e_conv_b, 4), ("ln_g", e_ln_g, 4),
                            ("ln_b", e_ln_b, 4), ("pool_scale", e_pool_scale, 4), ("norm2", e_norm2, 8),
                            ("onorm1", o_norm1, 8), ("b_qk", o_b_qkv, 12), ("b_o", o_b_o, 8),
                            ("onorm2", o_norm2, 8)):
            VEC[name] = (at, n, ap)
            at += n

        def col(name, k):
            return vec[:, VEC[name][0] + k:VEC[name][0] + k + 1]

        eps_ready = sem("eps_ready")
        x_loaded = sem("x_loaded")
        small_loaded = sem("small_loaded")
        bv_loaded = sem("bv_loaded")
        fnorm_loaded = sem("fnorm_loaded")
        win_loaded = [sem(f"win_loaded{c}") for c in range(KC + 1)]
        wout_loaded = [sem(f"wout_loaded{c}") for c in range(2)]
        ff_loaded = [sem(f"ff_loaded{u}") for u in range(FF_UNITS)]
        qkv_loaded = sem("qkv_loaded")
        wo_loaded = sem("wo_loaded")
        up_loaded = [sem(f"up_loaded{s}") for s in range(UPS)]
        down_loaded = [sem(f"down_loaded{s}") for s in range(DOWNS)]
        const_step = sem("const_step")
        consts = sem("consts")
        pads = sem("pads")
        xT_done = sem("xT_done")
        vecT_done = sem("vecT_done")
        vec_ready = sem("vec_ready")
        res_ready = [sem(f"res_ready{n}") for n in range(4)]
        sq_ready = [sem(f"sq_ready{n}") for n in range(4)]
        ss_done = [sem(f"ss_done{n}") for n in range(4)]
        std_ready = [sem(f"std_ready{n}") for n in range(4)]
        rstd_ready = [sem(f"rstd_ready{n}") for n in range(4)]
        hn_ready = [sem(f"hn_ready{n}") for n in range(4)]
        u_done = sem("u_done")
        sig_ready = sem("sig_ready")
        glu_ready = sem("glu_ready")
        b_done = sem("b_done")
        b_ready = sem("b_ready")
        pool_step = sem("pool_step")
        pool_ready = sem("pool_ready")
        pmap_done = sem("pmap_done")
        pmix_ready = sem("pmix_ready")
        conv_step = sem("conv_step")
        conv_ready = sem("conv_ready")
        mean_done = sem("mean_done")
        cent_ready = sem("cent_ready")
        lsq_ready = sem("lsq_ready")
        var_done = sem("var_done")
        lstd_ready = sem("lstd_ready")
        lrstd_ready = sem("lrstd_ready")
        ln_ready = sem("ln_ready")
        cmix_ready = sem("cmix_ready")
        wout_done = sem("wout_done")
        ff_h_done = sem("ff_h_done")
        ff_sg_ready = sem("ff_sg_ready")
        ff_h_ready = sem("ff_h_ready")
        ff_down_done = sem("ff_down_done")
        ff_added = sem("ff_added")
        k_done = sem("k_done")
        v_done = sem("v_done")
        q_done = sem("q_done")
        k_half = sem("k_half")
        k_ready = sem("k_ready")
        v_ready = sem("v_ready")
        q_ready = sem("q_ready")
        s_done = sem("s_done")
        s_masked = sem("s_masked")
        neg_ready = sem("neg_ready")
        e_ready = sem("e_ready")
        den_step = sem("den_step")
        p_ready = sem("p_ready")
        pT_done = sem("pT_done")
        pT_dve = sem("pT_dve")
        pT_act = sem("pT_act")
        o_done = sem("o_done")
        o_ready = sem("o_ready")
        wo_done = sem("wo_done")
        logit_done = sem("logit_done")
        tN_done = sem("tN_done")
        tN_ready = sem("tN_ready")
        acc_done = sem("acc_done")
        acc_ready = sem("acc_ready")
        route = sem("route")
        top_ready = sem("top_ready")
        ratio_ready = sem("ratio_ready")
        chosen_ready = sem("chosen_ready")
        place_done = sem("place_done")
        jobs_ready = sem("jobs_ready")
        sel_ready = sem("sel_ready")
        gathered = sem("gathered")
        xg_act = sem("xg_act")
        xg_dve = sem("xg_dve")
        selT_done = sem("selT_done")
        selT_ready = sem("selT_ready")
        h_done = sem("h_done")
        sg_ready = sem("sg_ready")
        h_ready = sem("h_ready")
        down_done = sem("down_done")
        y_zero = sem("y_zero")
        y_added = sem("y_added")
        yT_done = sem("yT_done")
        ys_ready = sem("ys_ready")
        back_done = sem("back_done")
        back_added = sem("back_added")
        ssq_ready = sem("ssq_ready")
        fstd_ready = sem("fstd_ready")
        frstd_ready = sem("frstd_ready")
        final_ready = sem("final_ready")
        stored = sem("stored")

        N_SMALL = len(VEC) + 4
        N_CONST = 6
        HEAD = 1

        block = ctx.enter_context(nc.Block())

        @block.sync
        def _(sp):
            sp.dma_start(nat[:, :, :], x[0].rearrange("(b p) d -> p b d", p=P)).then_inc(x_loaded, 16)
            w_in_d = e_w_in[0].rearrange("(k p) n -> p k n", p=P)
            for c in range(KC):
                for part_at in (c * P, D_CONV + c * P):
                    sp.dma_start(w_in[:, :, part_at:part_at + P],
                                 w_in_d[:, :, part_at:part_at + P]).then_inc(win_loaded[c], 16)
            sp.dma_start(w_in[:, :, 2 * D_CONV:], w_in_d[:, :, 2 * D_CONV:]).then_inc(win_loaded[KC], 16)
            w_out_d = e_w_out[0].rearrange("(k p) n -> p k n", p=P)
            for c in range(2):
                k0 = (1 - c) * 4
                sp.dma_start(w_out[:, k0:k0 + 4, :], w_out_d[:, k0:k0 + 4, :]).then_inc(wout_loaded[c], 16)

            ff_d = [w[0].rearrange("(k p) (f n) -> p k f n", p=P, n=P) for w in (e_ff_w1, e_ff_w3)]
            ff_d2 = e_ff_w2[0].rearrange("(f p) n -> p f n", p=P)

            def load_ff(f):
                u = ff_unit[f % FF_UNITS]
                for i in range(2):
                    sp.dma_start(ff_up[u][:, i], ff_d[i][:, :, f, :]).then_inc(ff_loaded[u], 16)
                sp.dma_start(ff_down[u], ff_d2[:, f, :]).then_inc(ff_loaded[u], 16)

            for f in range(FF):
                if f == 5:
                    sp.wait_ge(b_done, NG)
                if f == 8:
                    sp.wait_ge(wout_done, 4)
                if f >= FF_UNITS:
                    sp.wait_ge(ff_down_done, HEAD + f - FF_UNITS + 1)
                load_ff(f)

            sp.wait_ge(ff_down_done, HEAD + FF_UNITS + 4)
            sp.dma_start(w_qkv[:, :, :], o_w_qkv[0].rearrange("(k p) n -> p k n", p=P)).then_inc(qkv_loaded, 16)
            sp.wait_ge(ff_down_done, HEAD + FF_UNITS + 7)
            sp.dma_start(w_o[:, :, :], o_w_o[0].rearrange("(k p) n -> p k n", p=P)).then_inc(wo_loaded, 16)

            up_d = [w[0].rearrange("e (k p) (g n) -> e g p k n", p=P, n=2 * P) for w in (o_exp_w1, o_exp_w3)]
            down_d = o_exp_w2[0].rearrange("e (f p) n -> e f p n", p=P)

            def load_up(e, half, g):
                for i in range(2):
                    src = up_d[i][bass.ds(e, 1), half * UPS + g]
                    sp.dma_start(exp_up[up_slot[g]][:, i], src.rearrange("e p k n -> p (e k) n")
                                 ).then_inc(up_loaded[up_slot[g]], 16)

            def load_down(e, half, i):
                s = down_slot[i % DOWNS]
                src = down_d[bass.ds(e, 1), half * HALF + i]
                sp.dma_start(exp_down[s], src.rearrange("e p n -> p (e n)")).then_inc(down_loaded[s], 16)

            sp.wait_ge(ff_down_done, HEAD + FF)
            for g in range(UPS):
                if g == 3:
                    sp.wait_ge(q_done, KD)
                if g == 5:
                    sp.wait_ge(wo_done, 4)
                load_up(0, 0, g)
                for i in (2 * g, 2 * g + 1):
                    if i < 3:
                        load_down(0, 0, i)
                if g == 3:
                    for i in range(3, DOWNS):
                        load_down(0, 0, i)
            for i in range(DOWNS, HALF):
                sp.wait_ge(down_done, HEAD + i - DOWNS + 1)
                load_down(0, 0, i)

            def load_round(e, half, rounds):
                for g in range(UPS):
                    sp.wait_ge(h_done, HALF * (rounds - 1) + 2 * g + 2)
                    load_up(e, half, g)
                    for i in (2 * g, 2 * g + 1):
                        sp.wait_ge(down_done, HEAD + HALF * rounds + i - DOWNS + 1)
                        load_down(e, half, i)

            load_round(0, 1, 1)
            sp.wait_ge(jobs_ready, 1)
            n_jobs = sp.value_load(jobs_i[0:1, 2, 0:1], min_val=NE, max_val=MAX_JOBS)
            with sp.Fori(1, n_jobs) as j:
                e = sp.value_load(jobs_i[0:1, 0, bass.ds(j, 1)], min_val=0, max_val=NE - 1)
                for half in range(2):
                    load_round(e, half, 2 * j + half)

            for b in range(NB):
                sp.wait_ge(final_ready, b + 1)
                sp.dma_start(out[0, b * P:(b + 1) * P, :], res[:, b, :]).then_inc(stored, 16)
            sp.wait_ge(stored, 16 * NB)

        @block.gpsimd
        def _(pool):
            for name, (at, n, ap) in VEC.items():
                rows = ap[0].rearrange("(r n) -> r n", n=P)[0:n]
                pool.dma_start(hn[at:at + n, 0, 0:P], rows).then_inc(small_loaded, 16)
            pool.dma_start(conv_rows, e_conv_w[0]).then_inc(small_loaded, 16)
            pool.dma_start(pool_w, e_pool_w[0].rearrange("g c d -> c g d")).then_inc(small_loaded, 16)
            pool.dma_start(sinks[:, :], o_sinks[0:1, :].broadcast_to([P, NH])).then_inc(small_loaded, 16)
            pool.dma_start(router[:, :, :], o_router[0].rearrange("(k p) e -> p k e", p=P)
                           ).then_inc(small_loaded, 16)

            steps = [0]

            def then(ins):
                steps[0] += 1
                ins.then_inc(const_step, 1)
                pool.wait_ge(const_step, steps[0])

            then(pool.memset(ident[:, :], 0.0))
            pool.affine_select(out=ident[:, :], in_=ident[:, :], compare_op=ALU.not_equal, fill=1.0, base=0,
                               pattern=[[-1, P]], channel_multiplier=1).then_inc(consts, 1)
            pool.memset(ones[:, :], 1.0).then_inc(consts, 1)
            for t in (glu[:, :, 0:PADC], pool_in[:, :, 0:PADP]):
                pool.memset(t, 0.0).then_inc(pads, 1)
            then(pool.memset(pool_t[:, :, 0:PADP], 0.0))
            then(pool.memset(tri[:, :], 1.0))
            pool.affine_select(out=tri[:, :], in_=tri[:, :], compare_op=ALU.is_gt, fill=0.0, base=0,
                               pattern=[[1, P]], channel_multiplier=-1).then_inc(consts, 1)
            then(pool.iota(iota_i, pattern=[[1, P]], base=0, channel_multiplier=0))
            pool.tensor_copy(iota_f[:, :], iota_i).then_inc(consts, 1)
            pool.wait_ge(consts, 4)
            for g in range(NG):
                w = float(2 << g)
                then(pool.tensor_scalar(inv_cnt[:, g, :], iota_f[:, 0:16], 1.0, w, ALU.add, ALU.min))
            pool.tensor_copy(iota_e, iota_f[:, 0:NE].unsqueeze(1).broadcast_to([P, NB, NE])).then_inc(consts, 1)
            pool.nop().then_inc(consts, 1)

            psteps = [0]

            def link(ins):
                psteps[0] += 1
                ins.then_inc(pool_step, 1)
                pool.wait_ge(pool_step, psteps[0])

            pool.wait_ge(vec_ready, 3)
            for g in range(NG):
                pool.wait_ge(b_ready, g + 1)
                cur = pool_in[:, g, :]
                for s in range(g + 1):
                    nxt = pool_t[:, s % 2, :]
                    lag = 1 << s
                    link(pool.tensor_tensor(nxt[:, PADP:], cur[:, PADP:], cur[:, PADP - lag:PADP + SEQ - lag],
                                            ALU.add))
                    cur = nxt
                link(pool.tensor_tensor(cur[:, PADP:PADP + 16], cur[:, PADP:PADP + 16], inv_cnt[:, g, :], ALU.mult))
                link(pool.tensor_scalar(cur[:, PADP + 16:], cur[:, PADP + 16:], 1.0 / (2 << g), None, ALU.mult))
                ins = pool.tensor_tensor(pool_in[:, g, PADP:], cur[:, PADP:], pool_in[:, g, PADP:], ALU.subtract)
                link(ins)
                pool.nop().then_inc(pool_ready, 1)

            pool.wait_ge(wout_done, 4)
            pool.dma_start(b_v, o_b_qkv[0:1, D_QKV - NKV * HD:]).then_inc(bv_loaded, 16)
            pool.memset(mask, 0.0).then_inc(const_step, 1)
            base = steps[0] + 1
            pool.wait_ge(const_step, base)
            for n, (mult, step) in enumerate(((1, -1), (-1, 1), (1, -1))):
                off = -1 if n == 1 else 0
                pool.affine_select(out=mask[:, n * P:(n + 1) * P], in_=mask[:, n * P:(n + 1) * P],
                                   compare_op=ALU.is_ge, fill=NEG, base=off, pattern=[[step, P]],
                                   channel_multiplier=mult).then_inc(const_step, 1)

            pool.wait_ge(acc_done, 4)
            pool.dma_start(fnorm, final_norm.rearrange("(a d) -> a d", a=1).broadcast_to([P, D])
                           ).then_inc(fnorm_loaded, 16)

        MASK_STEPS = 1 + 2 + 1 + NG + 4

        @block.tensor
        def _(pe):
            def sum_squares(n, bank):
                for k in range(KD):
                    if k % 2 == 0:
                        pe.wait_ge(sq_ready[n], k // 2 + 1)
                    mm = pe.matmul(PS[:, bank, 0:SEQ], ones[:, :], sq[:, k, :], start=(k == 0), stop=(k == KD - 1))
                mm.then_inc(ss_done[n], 1)

            for s in (ff_down_done, down_done, yT_done, back_done):
                pe.sem_inc(s, HEAD)

            pe.wait_ge(consts, 2)
            pe.wait_ge(x_loaded, 16)
            for i in range(4):
                for kk in range(2):
                    for b in range(NB):
                        k = 2 * i + kk
                        mm = pe.transpose(PS[:, i, (kk * 2 + b) * P:(kk * 2 + b + 1) * P],
                                          nat[:, b, k * P:(k + 1) * P], ident[:, :])
                mm.then_inc(xT_done, 1)
            pe.wait_ge(small_loaded, 16 * N_SMALL)
            pe.transpose(PS[:, 4, 0:68], vec_rows, ident[0:68, 0:68])
            for c in range(KC):
                mm = pe.transpose(PS[:, 4, 128 + 32 * c:128 + 32 * c + CONV_K], conv_rows[:, c * P:(c + 1) * P],
                                  ident[0:CONV_K, 0:CONV_K])
            mm.then_inc(vecT_done, 1)
            sum_squares(0, 7)

            for c in range(KC):
                pe.wait_ge(win_loaded[c], 32)
                for i in range(2):
                    at = i * D_CONV + c * P
                    for k in range(KD):
                        if c == 0 and i == 0:
                            pe.wait_ge(hn_ready[0], k + 1)
                        mm = pe.matmul(PS[:, c, i * SEQ:(i + 1) * SEQ], w_in[:, k, at:at + P], hn[:, k, :],
                                       start=(k == 0), stop=(k == KD - 1))
                mm.then_inc(u_done, 1)
            pe.wait_ge(win_loaded[KC], 16)
            for g in range(NG):
                at = 2 * D_CONV + g * P
                for k in range(KD):
                    mm = pe.matmul(PS[:, 4 + g, 0:SEQ], w_in[:, k, at:at + P], hn[:, k, :],
                                   start=(k == 0), stop=(k == KD - 1))
                mm.then_inc(b_done, 1)
            for g in range(NG):
                pe.wait_ge(pool_ready, g + 1)
                pe.matmul(PS[:, 4 + g, SEQ:2 * SEQ], pool_w[:, g, :], pool_in[:, g, PADP:],
                          start=True, stop=True).then_inc(pmap_done, 1)
            pe.wait_ge(wout_loaded[0], 16)
            pe.wait_ge(glu_ready, KC)
            pe.wait_ge(pmix_ready, NG)
            for m in range(KD):
                for k in range(4, KD):
                    pe.matmul(PS[:, 2 + m // 2, (m % 2) * SEQ:(m % 2 + 1) * SEQ], w_out[:, k, m * P:(m + 1) * P],
                              mix[:, k, :], start=(m % 2 == 0 and k == 4), stop=False, skip_group_check=True)
            for c in range(KC):
                pe.wait_ge(conv_ready, c + 1)
                mm = pe.matmul(PS[:, 0, 0:SEQ], ones[:, :], conv[:, c, :], start=(c == 0), stop=(c == KC - 1))
            mm.then_inc(mean_done, 1)
            for c in range(KC):
                pe.wait_ge(lsq_ready, c + 1)
                mm = pe.matmul(PS[:, 1, 0:SEQ], ones[:, :], sq[:, c, :], start=(c == 0), stop=(c == KC - 1))
            mm.then_inc(var_done, 1)
            pe.wait_ge(wout_loaded[1], 16)
            for m in range(KD):
                for k in range(KC):
                    if m == 0:
                        pe.wait_ge(cmix_ready, k + 1)
                    mm = pe.matmul(PS[:, 2 + m // 2, (m % 2) * SEQ:(m % 2 + 1) * SEQ],
                                   w_out[:, k, m * P:(m + 1) * P], mix[:, k, :], start=False,
                                   stop=(k == KC - 1), skip_group_check=True)
                if m % 2:
                    mm.then_inc(wout_done, 1)
            sum_squares(1, 7)

            with pe.Fori(0, 2) as r:
                def up(j):
                    if r_first[0]:
                        r_first[0] = False
                        pe.wait_ge(hn_ready[1], KD)
                    pe.wait_ge(ff_loaded[ff_unit[j]], 48 * r + 48)
                    pe.wait_ge(ff_h_ready, HEAD + FF_UNITS * r + (j - 1 if j >= 2 else 0))
                    for i in range(2):
                        for k in range(KD):
                            mm = pe.matmul(PS[:, 4 + j % 2, i * SEQ:(i + 1) * SEQ], ff_up[ff_unit[j]][:, i, k, :],
                                           hn[:, k, :], start=(k == 0), stop=(k == KD - 1))
                    mm.then_inc(ff_h_done, 1)

                def down(j):
                    pe.wait_ge(ff_h_ready, HEAD + FF_UNITS * r + j + 1)
                    if j == 0:
                        pe.wait_ge(ff_added, HEAD + 4 * r)
                    for m in range(KD):
                        mm = pe.matmul(PS[:, m // 2, (m % 2) * SEQ:(m % 2 + 1) * SEQ],
                                       ff_down[ff_unit[j]][:, m * P:(m + 1) * P], ff_h[:, j % 2, :],
                                       start=(j == 0 and m % 2 == 0), stop=(j == FF_UNITS - 1),
                                       skip_group_check=True)
                    mm.then_inc(ff_down_done, 1)

                r_first = [True]
                up(0)
                for j in range(FF_UNITS):
                    if j + 1 < FF_UNITS:
                        up(j + 1)
                    down(j)
            sum_squares(2, 7)

            pe.wait_ge(qkv_loaded, 16)
            for m in range(2):
                at = D + m * P
                for k in range(KD):
                    if m == 0:
                        pe.wait_ge(hn_ready[2], k + 1)
                    mm = pe.matmul(PS[:, m, 0:SEQ], w_qkv[:, k, at:at + P], hn[:, k, :],
                                   start=(k == 0), stop=(k == KD - 1))
                mm.then_inc(k_done, 1)
            pe.wait_ge(bv_loaded, 16)
            for b in range(NB):
                for k in range(KD):
                    pe.matmul(PS[:, 2 + b, 0:NKV * HD], hn[:, k, b * P:(b + 1) * P], w_qkv[:, k, D + 2 * P:],
                              start=(k == 0), stop=False)
                pe.matmul(PS[:, 2 + b, 0:NKV * HD], ones[0:1, :], b_v, start=False, stop=True
                          ).then_inc(v_done, 1)

            def queries(m):
                if m >= 2:
                    pe.wait_ge(q_ready, m - 1)
                for k in range(KD):
                    mm = pe.matmul(PS[:, 4 + m % 2, 0:SEQ], w_qkv[:, k, m * P:(m + 1) * P], hn[:, k, :],
                                   start=(k == 0), stop=(k == KD - 1))
                mm.then_inc(q_done, 1)

            def scores(m):
                pe.wait_ge(q_ready, m + 1)
                pe.wait_ge(k_ready, NKV)
                for i in range(2):
                    h, j = 2 * m + i, (2 * m + i) // (NH // NKV)
                    if h >= 2:
                        pe.wait_ge(s_masked, h - 1)
                    r0 = HD * i
                    pe.matmul(PS[:, 6 + i, 0:P], q[r0:r0 + HD, m, 0:P], kT[r0:r0 + HD, j, 0:P],
                              start=True, stop=True)
                    pe.matmul(PS[:, 6 + i, P:3 * P], q[r0:r0 + HD, m, P:2 * P], kT[r0:r0 + HD, j, 0:2 * P],
                              start=True, stop=True).then_inc(s_done, 1)

            def turn_probs(m):
                pe.wait_ge(p_ready, m + 1)
                if m == 0:
                    pe.wait_ge(k_ready, NKV)
                else:
                    pe.wait_ge(pT_dve, m)
                    pe.wait_ge(pT_act, m)
                for i in range(2):
                    h = 2 * m + i
                    for n in range(3):
                        mm = pe.transpose(PS[:, i, n * P:(n + 1) * P], probs[:, h % 4, n * P:(n + 1) * P],
                                          ident[:, :])
                    mm.then_inc(pT_done, 1)

            def values(m):
                if m >= 2:
                    pe.wait_ge(o_ready, m - 1)
                else:
                    pe.wait_ge(v_ready, NB)
                pe.wait_ge(pT_dve, m + 1)
                pe.wait_ge(pT_act, m + 1)
                for i in range(2):
                    h = 2 * m + i
                    j = h // (NH // NKV)
                    dst = PS[HD * i:HD * (i + 1), 2 + m % 2, :]
                    v0, v1 = (vN[:, b, j * HD:(j + 1) * HD] for b in range(NB))
                    pe.matmul(dst[:, 0:P], v0, probsT[:, h % 4, 0:P], start=True, stop=True)
                    pe.matmul(dst[:, P:2 * P], v0, probsT[:, h % 4, P:2 * P], start=True, stop=False)
                    mm = pe.matmul(dst[:, P:2 * P], v1, probsT[:, h % 4, 2 * P:3 * P], start=False, stop=True)
                mm.then_inc(o_done, 1)

            for s in range(KD + 3):
                if s < KD:
                    queries(s)
                if 0 <= s - 1 < KD:
                    scores(s - 1)
                if 0 <= s - 2 < KD:
                    turn_probs(s - 2)
                if 0 <= s - 3 < KD:
                    values(s - 3)

            pe.wait_ge(wo_loaded, 16)
            pe.wait_ge(s_masked, NH)
            for m in range(KD):
                for k in range(KD):
                    if m == 0:
                        pe.wait_ge(o_ready, k + 1)
                    mm = pe.matmul(PS[:, 4 + m // 2, (m % 2) * SEQ:(m % 2 + 1) * SEQ], w_o[:, k, m * P:(m + 1) * P],
                                   oT[:, k, :], start=(k == 0), stop=(k == KD - 1))
                if m % 2:
                    mm.then_inc(wo_done, 1)
            sum_squares(3, 0)

            for i in range(4):
                b, half = divmod(i, 2)
                if i >= 2:
                    pe.wait_ge(acc_ready, i - 1)
                else:
                    pe.wait_ge(res_ready[3], 4)
                for kk in range(4):
                    mm = pe.transpose(PS[:, 6 + i % 2, kk * P:(kk + 1) * P],
                                      hT[:, half * 4 + kk, b * P:(b + 1) * P], ident[:, :])
                mm.then_inc(acc_done, 1)
            for b in range(NB):
                for k in range(KD):
                    if b == 0:
                        pe.wait_ge(hn_ready[3], k + 1)
                    mm = pe.matmul(PS[:, 1, b * NE:(b + 1) * NE], hn[:, k, b * P:(b + 1) * P], router[:, k, :],
                                   start=(k == 0), stop=(k == KD - 1))
            mm.then_inc(logit_done, 1)
            for i in range(4):
                b, half = divmod(i, 2)
                for kk in range(4):
                    mm = pe.transpose(PS[:, 2 + i, kk * P:(kk + 1) * P],
                                      hn[:, half * 4 + kk, b * P:(b + 1) * P], ident[:, :])
                mm.then_inc(tN_done, 1)
            pe.wait_ge(chosen_ready, 1)
            pe.matmul(PS[:, 1, 32:32 + NE], tri[:, :], chosen[:, 0, :], start=True, stop=True)
            pe.matmul(PS[:, 1, 32 + NE:32 + 2 * NE], ones[:, :], chosen[:, 0, :], start=True, stop=False)
            pe.matmul(PS[:, 1, 32 + NE:32 + 2 * NE], tri[:, :], chosen[:, 1, :], start=False, stop=True)
            pe.matmul(PS[:, 1, 64:64 + NE], ones[:, :], chosen[:, 0, :], start=True, stop=False)
            pe.matmul(PS[:, 1, 64:64 + NE], ones[:, :], chosen[:, 1, :], start=False, stop=True
                      ).then_inc(place_done, 1)

            def gather(j):
                pe.wait_ge(sel_ready, j + 1)
                for m in range(KD):
                    for b in range(NB):
                        mm = pe.matmul(PS[:, 6 + m // 4, (m % 4) * P:(m % 4 + 1) * P],
                                       tN[:, b, m * P:(m + 1) * P], sel[:, b, :],
                                       start=(b == 0), stop=(b == NB - 1))
                    if m % 4 == 3:
                        mm.then_inc(gathered, 1)

            def turn_sel():
                for b in range(NB):
                    mm = pe.transpose(PS[:, 6, b * P:(b + 1) * P], sel[:, b, :], ident[:, :])
                mm.then_inc(selT_done, 1)

            def expert(j, n):
                with pe.Fori(0, 2) as half:
                    rounds = 2 * j + half

                    def up(i):
                        slot = up_slot[i // 2]
                        if i % 2 == 0:
                            pe.wait_ge(up_loaded[slot], 32 * rounds + 32)
                        if i == 0:
                            pe.wait_ge(xg_act, j + 1)
                            pe.wait_ge(xg_dve, j + 1)
                        pe.wait_ge(h_ready, HEAD + HALF * rounds + (i - 1 if i >= 2 else 0))
                        for w in range(2):
                            for k in range(KD):
                                mm = pe.matmul(PS[:, 4 + i % 2, w * n:(w + 1) * n],
                                               exp_up[slot][:, w, k, (i % 2) * P:(i % 2 + 1) * P],
                                               xg[:, k, 0:n], start=(k == 0), stop=(k == KD - 1))
                        mm.then_inc(h_done, 1)

                    def down(i):
                        slot = down_slot[i % DOWNS]
                        pe.wait_ge(down_loaded[slot], 32 * rounds + 16 * (i // DOWNS + 1))
                        if i == 0:
                            pe.wait_ge(y_added, HEAD + 2 * rounds)
                            pe.wait_ge(ys_ready, HEAD + 2 * j)
                        pe.wait_ge(h_ready, HEAD + HALF * rounds + i + 1)
                        for m in range(KD):
                            mm = pe.matmul(PS[:, m // 4, (m % 4) * P:(m % 4) * P + n],
                                           exp_down[slot][:, m * P:(m + 1) * P], exp_h[:, i % 2, 0:n],
                                           start=(i == 0 and m % 4 == 0), stop=(i == HALF - 1),
                                           skip_group_check=True)
                        mm.then_inc(down_done, 1)

                    up(0)
                    for i in range(HALF):
                        if i + 1 < HALF:
                            up(i + 1)
                        down(i)

            pe.wait_ge(tN_ready, 4)
            pe.wait_ge(acc_ready, 4)
            gather(0)
            pe.wait_ge(xg_act, 1)
            pe.wait_ge(xg_dve, 1)
            turn_sel()
            pe.wait_ge(jobs_ready, 1)
            n_jobs = pe.value_load(jobs_i[0:1, 2, 0:1], min_val=NE, max_val=MAX_JOBS)
            with pe.Fori(0, n_jobs) as j:
                expert(j, JOB)
                pe.wait_ge(selT_ready, j + 1)
                gather(j + 1)
                pe.wait_ge(y_added, HEAD + 4 * j + 4)
                for m in range(KD):
                    mm = pe.transpose(PS[:, m // 4, (m % 4) * P:(m % 4 + 1) * P], yT[:, m, :], ident[:, :])
                    if m % 4 == 3:
                        mm.then_inc(yT_done, 1)
                for b in range(NB):
                    for half in range(2):
                        if b == 0:
                            pe.wait_ge(ys_ready, HEAD + 2 * j + half + 1)
                            pe.wait_ge((xg_act, xg_dve)[half], j + 2)
                        else:
                            pe.wait_ge(back_added, 4 * j + half + 1)
                        pe.matmul(PS[:, 6 + half, :], selT[:, b * P:(b + 1) * P],
                                  ys[:, half * 512:(half + 1) * 512], start=True, stop=True
                                  ).then_inc(back_done, 1)
                pe.wait_ge(back_added, 4 * j + 3)
                turn_sel()

        @block.scalar
        def _(act):
            def squares(n):
                for i in range(4):
                    act.wait_ge(res_ready[n], i + 1)
                    act.activation(sq[:, 2 * i:2 * i + 2, :], hT[:, 2 * i:2 * i + 2, :], ACT.Square
                                   ).then_inc(sq_ready[n], 1)

            def root(n, bank):
                act.wait_ge(ss_done[n], 1)
                act.activation(std[:, :], PS[:, bank, 0:SEQ], ACT.Sqrt, scale=1.0 / D, bias=eps[:, 0:1]
                               ).then_inc(std_ready[n], 1)

            act.sem_inc(ys_ready, HEAD)
            act.wait_ge(eps_ready, 1)
            squares(0)
            root(0, 7)
            for c in range(KC):
                act.wait_ge(u_done, c + 1)
                if c >= 2:
                    act.wait_ge(glu_ready, c - 1)
                act.activation(sig[:, c % 2, :], PS[:, c, SEQ:2 * SEQ], ACT.Sigmoid).then_inc(sig_ready, 1)
            act.wait_ge(pads, 2)
            for g in range(NG):
                act.wait_ge(b_done, g + 1)
                act.activation(pool_in[:, g, PADP:], PS[:, 4 + g, 0:SEQ], ACT.Copy).then_inc(b_ready, 1)
            for g in range(NG):
                act.wait_ge(pmap_done, g + 1)
                act.activation(mix[:, 4 + g, :], PS[:, 4 + g, SEQ:2 * SEQ], ACT.Copy,
                               scale=col("pool_scale", g)).then_inc(pmix_ready, 1)
            for c in range(KC):
                act.wait_ge(cent_ready, c + 1)
                act.activation(sq[:, c, :], conv[:, c, :], ACT.Square).then_inc(lsq_ready, 1)
            act.wait_ge(var_done, 1)
            act.activation(std[:, :], PS[:, 1, 0:SEQ], ACT.Sqrt, scale=1.0 / D_CONV, bias=eps[:, 0:1]
                           ).then_inc(lstd_ready, 1)
            for c in range(KC):
                act.wait_ge(ln_ready, c + 1)
                act.activation(mix[:, c, :], conv[:, c, :], ACT.Silu, bias=col("ln_b", c)).then_inc(cmix_ready, 1)
            squares(1)
            root(1, 7)

            with act.Fori(0, 2) as r:
                for j in range(FF_UNITS):
                    act.wait_ge(ff_h_done, FF_UNITS * r + j + 1)
                    act.wait_ge(ff_h_ready, HEAD + FF_UNITS * r + (j - 1 if j >= 2 else 0))
                    act.activation(ff_sg[:, j % 2, :], PS[:, 4 + j % 2, 0:SEQ], ACT.Silu).then_inc(ff_sg_ready, 1)

            squares(2)
            root(2, 7)

            for m in range(2):
                act.wait_ge(k_done, m + 1)
                for i in range(2):
                    r0 = HD * i
                    act.activation(kT[r0:r0 + HD, 2 * m + i, :], PS[r0:r0 + HD, m, 0:SEQ], ACT.Identity,
                                   bias=vec[r0:r0 + HD, VEC["b_qk"][0] + KD + m:VEC["b_qk"][0] + KD + m + 1]
                                   ).then_inc(k_half, 1)
            for b in range(NB):
                act.wait_ge(v_done, b + 1)
                act.activation(vN[:, b, :], PS[:, 2 + b, 0:NKV * HD], ACT.Copy).then_inc(v_ready, 1)

            for s in range(KD + 3):
                if s < KD:
                    act.wait_ge(q_done, s + 1)
                    act.activation(q[:, s, :], PS[:, 4 + s % 2, 0:SEQ], ACT.Identity, bias=col("b_qk", s)
                                   ).then_inc(q_ready, 1)
                if 0 <= s - 2 < KD:
                    m = s - 2
                    act.wait_ge(pT_done, 2 * m + 2)
                    if m >= 2:
                        act.wait_ge(o_done, m - 1)
                    act.activation(probsT[:, (2 * m + 1) % 4, :], PS[:, 1, 0:3 * P], ACT.Copy).then_inc(pT_act, 1)
                if 0 <= s - 3 < KD:
                    m = s - 3
                    act.wait_ge(o_done, m + 1)
                    act.activation(oT[:, m, :], PS[:, 2 + m % 2, 0:SEQ], ACT.Copy).then_inc(o_ready, 1)
                if 0 <= s - 1 < KD:
                    m = s - 1
                    act.wait_ge(neg_ready, m + 1)
                    for i in range(2):
                        h = 2 * m + i
                        for n, (a, z) in enumerate(((0, P), (P, 3 * P))):
                            c = 2 * h + n
                            act.activation(probs[:, h % 4, a:z], probs[:, h % 4, a:z], ACT.Exp,
                                           bias=negm[:, c:c + 1], accum_out=rsum[:, c:c + 1])
                        last = act.activation(esink[:, 2 * h:2 * h + 2], negm[:, 2 * h:2 * h + 2], ACT.Exp,
                                              bias=sinks[:, h:h + 1])
                    last.then_inc(e_ready, 1)
            act.wait_ge(pT_done, NH)
            squares(3)
            root(3, 0)
            for i in range(4):
                act.wait_ge(tN_done, i + 1)
                if i == 0:
                    act.wait_ge(ss_done[3], 1)
                b, half = divmod(i, 2)
                act.activation(tN[:, b, half * 512:(half + 1) * 512], PS[:, 2 + i, :], ACT.Copy
                               ).then_inc(tN_ready, 1)
            act.wait_ge(top_ready, 1)
            act.activation(ratio, arg, ACT.Exp).then_inc(ratio_ready, 1)

            def take_gathered(j):
                act.wait_ge(gathered, 2 * j + 1)
                act.activation(xg[:, 0:4, :], PS[:, 6, :].rearrange("p (k n) -> p k n", n=P), ACT.Copy
                               ).then_inc(xg_act, 1)

            def expert(j, n):
                with act.Fori(0, 2) as half:
                    rounds = 2 * j + half
                    for i in range(HALF):
                        act.wait_ge(h_done, HALF * rounds + i + 1)
                        act.wait_ge(h_ready, HEAD + HALF * rounds + (i - 1 if i >= 2 else 0))
                        act.activation(exp_sg[:, i % 2, 0:n], PS[:, 4 + i % 2, 0:n], ACT.Silu
                                       ).then_inc(sg_ready, 1)

            take_gathered(0)
            act.wait_ge(jobs_ready, 1)
            n_jobs = act.value_load(jobs_i[0:1, 2, 0:1], min_val=NE, max_val=MAX_JOBS)
            with act.Fori(0, n_jobs) as j:
                expert(j, JOB)
                take_gathered(j + 1)
                for half in range(2):
                    act.wait_ge(yT_done, HEAD + 2 * j + half + 1)
                    if half == 0:
                        act.wait_ge(back_done, HEAD + 4 * j)
                    act.activation(ys[:, half * 512:(half + 1) * 512], PS[:, half, :], ACT.Copy
                                   ).then_inc(ys_ready, 1)
            act.wait_ge(back_added, 4 * n_jobs)
            for b in range(NB):
                act.activation(res[:, b, :], nat[:, b, :], ACT.Square, accum_out=ssq[:, b:b + 1]
                               ).then_inc(ssq_ready, 1)
            act.wait_ge(ssq_ready, NB)
            act.activation(frstd, ssq, ACT.Sqrt, scale=1.0 / D, bias=eps[:, 0:1]).then_inc(fstd_ready, 1)

        @block.vector
        def _(dve):
            def normed(n, gain, dst):
                dve.wait_ge(std_ready[n], 1)
                dve.reciprocal(rstd[:, :], std[:, :]).then_inc(rstd_ready[n], 1)
                dve.wait_ge(rstd_ready[n], 1)
                for k in range(KD):
                    dve.scalar_tensor_tensor(out=dst[:, k, :], in0=hT[:, k, :], scalar=col(gain, k), in1=rstd[:, :],
                                             op0=ALU.mult, op1=ALU.mult).then_inc(hn_ready[n], 1)

            for s in (ff_h_ready, ff_added, h_ready, y_added):
                dve.sem_inc(s, HEAD)
            dve.memset(eps[:, :], RMS_EPS).then_inc(eps_ready, 1)
            for i in range(4):
                dve.wait_ge(xT_done, i + 1)
                dve.tensor_copy(hT[:, 2 * i:2 * i + 2, :], PS[:, i, :].rearrange("p (k n) -> p k n", n=SEQ)
                                ).then_inc(res_ready[0], 1)
            dve.wait_ge(vecT_done, 1)
            dve.tensor_copy(vec[:, :], PS[:, 4, 0:68]).then_inc(vec_ready, 1)
            dve.tensor_copy(conv_w[:, :, :], PS[:, 4, 128:256].rearrange("p (c n) -> p c n", n=32)[:, :, 0:CONV_K]
                            ).then_inc(vec_ready, 1)
            dve.wait_ge(consts, N_CONST)
            dve.reciprocal(inv_cnt[:, :, :], inv_cnt[:, :, :]).then_inc(vec_ready, 1)
            dve.wait_ge(vec_ready, 3)
            normed(0, "norm1", hn)

            steps = [0]

            def tap(ins, after=None):
                steps[0] += 1
                ins.then_inc(conv_step, 1)

            dve.wait_ge(pads, 2)
            for c in range(KC):
                dve.wait_ge(sig_ready, c + 1)
                dve.tensor_tensor(glu[:, c, PADC:], PS[:, c, 0:SEQ], sig[:, c % 2, :], ALU.mult
                                  ).then_inc(glu_ready, 1)
                dve.wait_ge(glu_ready, c + 1)
                if c:
                    dve.wait_ge(conv_ready, c)
                for j in range(CONV_K):
                    acc = conv[:, c, :] if j % 2 == 0 else conv_b2
                    src, w = glu[:, c, j:j + SEQ], conv_w[:, c, j:j + 1]
                    if j == 0:
                        tap(dve.tensor_scalar(acc, src, w, col("conv_b", c), ALU.mult, ALU.add))
                    elif j == 1:
                        tap(dve.tensor_scalar(acc, src, w, None, ALU.mult))
                    else:
                        dve.wait_ge(conv_step, steps[0] - 1)
                        tap(dve.scalar_tensor_tensor(out=acc, in0=src, scalar=w, in1=acc, op0=ALU.mult, op1=ALU.add))
                dve.wait_ge(conv_step, steps[0])
                dve.tensor_tensor(conv[:, c, :], conv[:, c, :], conv_b2, ALU.add).then_inc(conv_ready, 1)

            dve.wait_ge(mean_done, 1)
            for c in range(KC):
                dve.scalar_tensor_tensor(out=conv[:, c, :], in0=PS[:, 0, 0:SEQ], scalar=-1.0 / D_CONV,
                                         in1=conv[:, c, :], op0=ALU.mult, op1=ALU.add).then_inc(cent_ready, 1)
            dve.wait_ge(lstd_ready, 1)
            dve.reciprocal(rstd[:, :], std[:, :]).then_inc(lrstd_ready, 1)
            dve.wait_ge(lrstd_ready, 1)
            dve.wait_ge(lsq_ready, KC)
            for c in range(KC):
                dve.scalar_tensor_tensor(out=conv[:, c, :], in0=conv[:, c, :], scalar=col("ln_g", c),
                                         in1=rstd[:, :], op0=ALU.mult, op1=ALU.mult).then_inc(ln_ready, 1)

            def add_bank(i, bank):
                return dve.tensor_tensor(hT[:, 2 * i:2 * i + 2, :], PS[:, bank, :].rearrange("p (k n) -> p k n", n=SEQ),
                                         hT[:, 2 * i:2 * i + 2, :], ALU.add)

            for i in range(4):
                dve.wait_ge(wout_done, i + 1)
                add_bank(i, 2 + i).then_inc(res_ready[1], 1)
            dve.wait_ge(res_ready[1], 4)
            normed(1, "norm2", hn)

            with dve.Fori(0, 2) as r:
                for j in range(FF_UNITS):
                    dve.wait_ge(ff_sg_ready, FF_UNITS * r + j + 1)
                    dve.wait_ge(ff_down_done, HEAD + FF_UNITS * r + (j - 1 if j >= 2 else 0))
                    dve.tensor_tensor(ff_h[:, j % 2, :], PS[:, 4 + j % 2, SEQ:2 * SEQ], ff_sg[:, j % 2, :], ALU.mult
                                      ).then_inc(ff_h_ready, 1)
                dve.wait_ge(ff_down_done, HEAD + FF_UNITS * r + FF_UNITS)
                dve.wait_ge(ff_added, HEAD + 4 * r)
                for i in range(4):
                    add_bank(i, i).then_inc(ff_added, 1)
            dve.wait_ge(ff_added, HEAD + 8)
            for i in range(4):
                dve.sem_inc(res_ready[2], 1)
            normed(2, "onorm1", hn)

            for j in range(NKV):
                dve.wait_ge(k_half, j + 1)
                a, z = (0, HD) if j % 2 == 0 else (HD, 2 * HD)
                dve.tensor_copy(kT[HD - a:2 * HD - a, j, :], kT[a:z, j, :]).then_inc(k_ready, 1)

            dve.wait_ge(const_step, MASK_STEPS)
            dve.wait_ge(small_loaded, 16 * N_SMALL)
            dsteps = [0]

            def link(ins):
                dsteps[0] += 1
                ins.then_inc(den_step, 1)
                dve.wait_ge(den_step, dsteps[0])

            for s in range(1, KD + 3):
                if 0 <= s - 2 < KD:
                    m = s - 2
                    c = slice(4 * m, 4 * m + 4)
                    dve.wait_ge(e_ready, m + 1)
                    link(dve.tensor_tensor(den[:, c], rsum[:, c], esink[:, c], ALU.add))
                    link(dve.reciprocal(rden[:, c], den[:, c]))
                    for i in range(2):
                        h = 2 * m + i
                        for n, (a, z) in enumerate(((0, P), (P, 3 * P))):
                            last = dve.tensor_scalar(probs[:, h % 4, a:z], probs[:, h % 4, a:z],
                                                     rden[:, 2 * h + n:2 * h + n + 1], None, ALU.mult)
                    last.then_inc(p_ready, 1)
                if 0 <= s - 1 < KD:
                    m = s - 1
                    for i in range(2):
                        h = 2 * m + i
                        dve.wait_ge(s_done, h + 1)
                        if h >= 4:
                            dve.wait_ge(pT_done, h - 3)
                        elif h == 0:
                            dve.wait_ge(ss_done[2], 1)
                        for n, (a, z) in enumerate(((0, P), (P, 3 * P))):
                            last = dve.tensor_tensor_reduce(
                                out=probs[:, h % 4, a:z], in0=PS[:, 6 + i, a:z], in1=mask[:, a:z], scale=SCALE,
                                scalar=sinks[:, h:h + 1], op0=ALU.add, op1=ALU.max,
                                accum_out=mx[:, 2 * h + n:2 * h + n + 1])
                        last.then_inc(s_masked, 1)
                    dve.wait_ge(s_masked, 2 * m + 2)
                    dve.tensor_scalar(negm[:, 4 * m:4 * m + 4], mx[:, 4 * m:4 * m + 4], -1.0, None, ALU.mult
                                      ).then_inc(neg_ready, 1)
                if 0 <= s - 2 < KD:
                    m = s - 2
                    dve.wait_ge(pT_done, 2 * m + 1)
                    if m >= 2:
                        dve.wait_ge(o_done, m - 1)
                    dve.tensor_copy(probsT[:, (2 * m) % 4, :], PS[:, 0, 0:3 * P]).then_inc(pT_dve, 1)

            for i in range(4):
                dve.wait_ge(wo_done, i + 1)
                for kk in range(2):
                    k = 2 * i + kk
                    last = dve.scalar_tensor_tensor(out=hT[:, k, :], in0=PS[:, 4 + i, kk * SEQ:(kk + 1) * SEQ],
                                                    scalar=col("b_o", k), in1=hT[:, k, :], op0=ALU.add, op1=ALU.add)
                last.then_inc(res_ready[3], 1)
            dve.wait_ge(res_ready[3], 4)
            for i in range(4):
                b, half = divmod(i, 2)
                dve.wait_ge(acc_done, i + 1)
                dve.tensor_copy(nat[:, b, half * 512:(half + 1) * 512], PS[:, 6 + i % 2, :]).then_inc(acc_ready, 1)
            normed(3, "onorm2", hn)

            rsteps = [0]

            def then(ins):
                rsteps[0] += 1
                ins.then_inc(route, 1)
                dve.wait_ge(route, rsteps[0])

            def wide(ap):
                return ap.unsqueeze(2).broadcast_to([P, NB, NE])

            def choose(values, top, which):
                then(dve.tensor_reduce(top, values, X, ALU.max))
                then(dve.tensor_tensor(less, values, wide(top), ALU.is_lt))
                then(dve.scalar_tensor_tensor(out=place, in0=less, scalar=float(2 * NE), in1=iota_e,
                                              op0=ALU.mult, op1=ALU.add))
                then(dve.tensor_reduce(arg, place, X, ALU.min))
                then(dve.tensor_tensor(which, iota_e, wide(arg), ALU.is_equal))

            dve.wait_ge(logit_done, 1)
            then(dve.tensor_copy(logits, PS[:, 1, 0:NB * NE].rearrange("p (b e) -> p b e", b=NB)))
            choose(logits, top1, first)
            then(dve.scalar_tensor_tensor(out=logits, in0=first, scalar=-3e38, in1=logits, op0=ALU.mult, op1=ALU.add))
            choose(logits, top2, second)
            dve.tensor_tensor(chosen, first, second, ALU.add).then_inc(chosen_ready, 1)
            dve.tensor_tensor(arg, top2, top1, ALU.subtract).then_inc(top_ready, 1)
            dve.wait_ge(ratio_ready, 1)
            then(dve.tensor_scalar(share2, ratio, 1.0, None, ALU.add))
            then(dve.reciprocal(share1, share2))
            then(dve.tensor_tensor(share2, ratio, share1, ALU.mult))
            then(dve.tensor_tensor(first, first, wide(share1), ALU.mult))
            then(dve.tensor_tensor(second, second, wide(share2), ALU.mult))
            then(dve.tensor_tensor(gates, first, second, ALU.add))

            dve.wait_ge(place_done, 1)
            dve.wait_ge(chosen_ready, 1)
            then(dve.scalar_tensor_tensor(out=slots, in0=PS[:, 1, 32:32 + NB * NE].rearrange("p (b e) -> p b e", b=NB),
                                          scalar=1.0, in1=chosen, op0=ALU.add, op1=ALU.mult))
            then(dve.tensor_scalar(slots, slots, -1.0, None, ALU.add))
            count, need, run, run2 = je[:, 0, 0:NE], je[:, 1, 0:NE], je[:, 2, 0:NE], je[:, 3, 0:NE]
            owner, begin, offs, left = je[:, 4, 0:NJ], je[:, 5, 0:NJ], je[:, 6, 0:NJ], je[:, 7, 0:NJ]
            then(dve.tensor_copy(count, PS[:, 1, 64:64 + NE]))
            then(dve.tensor_scalar(need, count, float(JOB), 1.0, ALU.is_gt, ALU.add))
            src, dst = need, run
            for s in (1, 2, 4):
                then(dve.tensor_copy(dst[:, 0:s], src[:, 0:s]))
                then(dve.tensor_tensor(dst[:, s:], src[:, s:], src[:, 0:NE - s], ALU.add))
                src, dst = dst, (run2 if dst is run else run)
            total = src[:, NE - 1:NE]
            then(dve.tensor_tensor(dst, src, need, ALU.subtract))
            start = dst
            by_job = [P, NJ, NE]

            def over_jobs(ap):
                return ap.unsqueeze(1).broadcast_to(by_job)

            def over_experts(ap):
                return ap.unsqueeze(2).broadcast_to(by_job)

            number = iota_f[:, 0:NJ]
            then(dve.tensor_tensor(jt[:, 0], over_experts(number), over_jobs(start), ALU.is_ge))
            then(dve.tensor_reduce(owner, jt[:, 0], X, ALU.add))
            then(dve.tensor_tensor(jt[:, 1], jt[:, 0], over_jobs(start), ALU.mult))
            then(dve.tensor_reduce(begin, jt[:, 1], X, ALU.max))
            then(dve.tensor_scalar(owner, owner, -1.0, None, ALU.add))
            then(dve.tensor_tensor(jt[:, 2], over_experts(owner), over_jobs(iota_f[:, 0:NE]), ALU.is_equal))
            then(dve.tensor_tensor(jt[:, 3], jt[:, 2], over_jobs(count), ALU.mult))
            then(dve.tensor_reduce(left, jt[:, 3], X, ALU.add))
            then(dve.tensor_tensor(offs, number, begin, ALU.subtract))
            then(dve.tensor_scalar(offs, offs, float(JOB), None, ALU.mult))
            then(dve.tensor_tensor(left, left, offs, ALU.subtract))
            then(dve.tensor_copy(jobs_i[0:1, 0, :], owner[0:1]))
            then(dve.tensor_copy(jobs_i[0:1, 1, :], left[0:1]))
            dve.tensor_copy(jobs_i[0:1, 2, 0:1], total[0:1]).then_inc(jobs_ready, 1)
            dve.wait_ge(jobs_ready, 1)

            def select(j, e):
                for b in range(NB):
                    last = dve.tensor_scalar(sel[:, b, :], iota_f[:, :], offs[:, bass.ds(j, 1)],
                                             slots[:, b, bass.ds(e, 1)], ALU.add, ALU.is_equal)
                last.then_inc(sel_ready, 1)

            def take_gathered(j):
                dve.wait_ge(gathered, 2 * j + 2)
                dve.tensor_copy(xg[:, 4:8, :], PS[:, 7, :].rearrange("p (k n) -> p k n", n=P)).then_inc(xg_dve, 1)

            def take_sel(j):
                dve.wait_ge(selT_done, j + 1)
                dve.tensor_copy(selT, PS[:, 6, 0:NB * P]).then_inc(selT_ready, 1)

            def expert(j, n):
                with dve.Fori(0, 2) as half:
                    rounds = 2 * j + half
                    for i in range(HALF):
                        dve.wait_ge(sg_ready, HALF * rounds + i + 1)
                        dve.wait_ge(down_done, HEAD + HALF * rounds + (i - 1 if i >= 2 else 0))
                        dve.tensor_tensor(exp_h[:, i % 2, 0:n], PS[:, 4 + i % 2, n:2 * n], exp_sg[:, i % 2, 0:n],
                                          ALU.mult).then_inc(h_ready, 1)
                    dve.wait_ge(down_done, HEAD + HALF * rounds + HALF)
                    dve.wait_ge(y_added, HEAD + 2 * rounds)
                    for i in range(2):
                        dve.tensor_tensor(yT[:, 4 * i:4 * i + 4, 0:n],
                                          PS[:, i, :].rearrange("p (k n) -> p k n", n=P)[:, :, 0:n],
                                          yT[:, 4 * i:4 * i + 4, 0:n], ALU.add).then_inc(y_added, 1)

            select(0, 0)
            take_gathered(0)
            take_sel(0)
            n_jobs = dve.value_load(jobs_i[0:1, 2, 0:1], min_val=NE, max_val=MAX_JOBS)
            dve.wait_ge(tN_done, 4)
            with dve.Fori(0, n_jobs) as j:
                e = dve.value_load(jobs_i[0:1, 0, bass.ds(j, 1)], min_val=0, max_val=NE - 1)
                e_next = dve.value_load(jobs_i[0:1, 0, bass.ds(j + 1, 1)], min_val=0, max_val=NE - 1)
                dve.wait_ge(yT_done, HEAD + 2 * j)
                dve.memset(yT, 0.0).then_inc(y_zero, 1)
                dve.wait_ge(y_zero, j + 1)
                select(j + 1, e_next)
                expert(j, JOB)
                take_gathered(j + 1)
                for b in range(NB):
                    for half in range(2):
                        dve.wait_ge(back_done, HEAD + 4 * j + 2 * b + half + 1)
                        dst = nat[:, b, half * 512:(half + 1) * 512]
                        dve.scalar_tensor_tensor(out=dst, in0=PS[:, 6 + half, :], scalar=gates[:, b, bass.ds(e, 1)],
                                                 in1=dst, op0=ALU.mult, op1=ALU.add).then_inc(back_added, 1)
                take_sel(j + 1)

            dve.wait_ge(fstd_ready, 1)
            dve.reciprocal(frstd, frstd).then_inc(frstd_ready, 1)
            dve.wait_ge(frstd_ready, 1)
            dve.wait_ge(fnorm_loaded, 16)
            for b in range(NB):
                dve.scalar_tensor_tensor(out=res[:, b, :], in0=nat[:, b, :], scalar=frstd[:, b:b + 1], in1=fnorm,
                                         op0=ALU.mult, op1=ALU.mult).then_inc(final_ready, 1)


_INS = ["x", "e_norm1", "e_w_in", "e_conv_w", "e_conv_b", "e_ln_g", "e_ln_b", "e_pool_w", "e_pool_scale",
        "e_w_out", "e_norm2", "e_ff_w1", "e_ff_w3", "e_ff_w2", "o_norm1", "o_w_qkv", "o_b_qkv", "o_sinks",
        "o_w_o", "o_b_o", "o_norm2", "o_router", "o_exp_w1", "o_exp_w3", "o_exp_w2", "final_norm"]


def kernel(**inputs):
    import numpy as _np
    import concourse.bacc as _bacc
    from concourse import mybir as _mybir
    from concourse.bass_utils import run_bass_kernel_spmd as _run

    nc = _bacc.Bacc("TRN2", target_bir_lowering=False, num_devices=1)
    arrays, args = {}, []
    for name in _INS:
        a = _np.ascontiguousarray(inputs[name])
        arrays[f"in_{name}_dram"] = a
        args.append(nc.dram_tensor(f"in_{name}_dram", a.shape, _mybir.dt.from_np(a.dtype), kind="ExternalInput").ap())
    shape = tuple(inputs["x"].shape)
    args.append(nc.dram_tensor("out_dram", shape, _mybir.dt.float32, kind="ExternalOutput").ap())
    hybrid_trunk(nc, *args)
    r = _run(nc, [arrays], core_ids=[0])
    return r.results[0]["out_dram"]
```

```python
from contextlib import ExitStack

import concourse.bass as bass
from concourse import mybir

F32 = mybir.dt.float32
F32R = mybir.dt.float32r
I32 = mybir.dt.int32
ALU = mybir.AluOpType
ACT = mybir.ActivationFunctionType
X = mybir.AxisListType.X

P = 128
KIB = 1024


def hybrid_trunk(nc, x, e_norm1, e_w_in, e_conv_w, e_conv_b, e_ln_g, e_ln_b, e_pool_w, e_pool_scale,
                 e_w_out, e_norm2, e_ff_w1, e_ff_w3, e_ff_w2, o_norm1, o_w_qkv, o_b_qkv, o_sinks,
                 o_w_o, o_b_o, o_norm2, o_router, o_exp_w1, o_exp_w3, o_exp_w2, final_norm, out):
    SEQ, D = x.shape[1], x.shape[2]
    NB = SEQ // P
    KD = D // P
    CONV_K, D_CONV = e_conv_w.shape[1], e_conv_w.shape[2]
    KC = D_CONV // P
    NG = e_pool_w.shape[1]
    D_IN = e_w_in.shape[2]
    FF = e_ff_w1.shape[2] // P
    NH = o_sinks.shape[1]
    NKV = 4
    HD = D // NH
    D_QKV = o_w_qkv.shape[2]
    NE = o_router.shape[2]
    FE = o_exp_w1.shape[3] // P
    RMS_EPS = LN_EPS = 1e-5
    SCALE = HD ** -0.5
    NEG = -1e30
    assert NB == 2 and KD == 8 and HD == 64 and NG == 4 and KC == 4

    JOB = P
    MAX_JOBS = NE + (2 * SEQ) // (JOB + 1)
    NJ = MAX_JOBS + 1
    GF = 4
    GROUPS = FE // GF
    UNIT = 4 * GF * P
    stream = []
    for g in range(GROUPS + 1):
        if g < GROUPS:
            stream += [("up", g, n) for n in range(4)]
        if g:
            stream += [("down", g - 1, n) for n in range(2)]
    UNITS = len(stream)
    RAW, SPLIT = 14, 3
    assert UNITS % RAW == 0 and UNITS % SPLIT == 0
    raw_slot = [(i + 10) % RAW for i in range(UNITS)]

    FFG = FF // 2
    FF_RAW = [11, 12, 13]

    W_BYTES = 140 * KIB
    W_OUT_AT = KD * D_IN * 4
    W_QKV_AT = 0
    W_O_AT = W_OUT_AT

    with ExitStack() as ctx:
        def sb(name, shape, dt=F32):
            return ctx.enter_context(nc.sbuf_tensor(name, shape, dt))

        def sem(name):
            return ctx.enter_context(nc.semaphore(name))

        BASE = (nc.sbuf_base + 31) // 32 * 32
        SPLIT_AT = RAW * UNIT * 4
        KEEP_AT = SPLIT_AT + 2 * SPLIT * UNIT * 4
        END = nc.sbuf_usable_end - BASE

        def at(name, offset, shape, dt=F32):
            n = 4
            for d in shape[1:]:
                n *= d
            assert offset + n <= END, (name, offset + n, END)
            return nc.alloc_sbuf_tensor_at(name, shape, dt, offset=BASE + offset)

        W = at("weights", 0, [P, W_BYTES // 4])
        raw = at("raw", 0, [P, RAW, UNIT])
        high = at("high", SPLIT_AT, [P, SPLIT, UNIT], F32R)
        low = at("low", SPLIT_AT + SPLIT * UNIT * 4, [P, SPLIT, UNIT], F32R)

        def w_at(at, *dims):
            n = 1
            for d in dims:
                n *= d
            names = "abcd"[:len(dims)]
            return W[:, at // 4:at // 4 + n].rearrange(
                f"p ({' '.join(names)}) -> p {' '.join(names)}", **{c: d for c, d in zip(names, dims)})

        w_in = w_at(0, KD, D_IN)
        w_out = w_at(W_OUT_AT, KD, D)
        w_qkv = w_at(W_QKV_AT, KD, D_QKV)
        w_o = w_at(W_O_AT, KD, D)
        PS = ctx.enter_context(nc.psum_tensor("banks", [P, 8, 512], F32))

        K8 = KD * SEQ * 4
        nat = at("natural", KEEP_AT, [P, NB, D])
        hT = at("residual_T", KEEP_AT + K8, [P, KD, SEQ])
        hn = at("normed_T", KEEP_AT + 2 * K8, [P, KD, SEQ])
        sq = at("squares", KEEP_AT + 3 * K8, [P, KD, SEQ])
        hn_high = at("hn_high", KEEP_AT, [P, KD, SEQ], F32R)
        hn_low = at("hn_low", KEEP_AT + 3 * K8, [P, KD, SEQ], F32R)
        x_high = at("x_high", KEEP_AT + K8, [P, KD, P], F32R)
        x_low = at("x_low", KEEP_AT + K8 + K8 // 2, [P, KD, P], F32R)
        h_high = at("h_high", KEEP_AT + 2 * K8, [P, GF, P], F32R)
        h_low = at("h_low", KEEP_AT + 2 * K8 + K8 // 4, [P, GF, P], F32R)
        gate_h = at("gate_h", KEEP_AT + 2 * K8 + K8 // 2, [P, GF * P])
        prod_h = at("prod_h", KEEP_AT + 2 * K8 + 3 * K8 // 4, [P, GF * P])
        fnorm = at("fnorm", KEEP_AT + K8, [P, D])
        AREA_B, AREA_C = KEEP_AT - W_BYTES, 2112 * 4
        area = {"b": at("area_b", W_BYTES, [P, AREA_B // 4]), "c": at("area_c", KEEP_AT + 4 * K8, [P, AREA_C // 4])}
        spot = [KEEP_AT + 4 * K8 + AREA_C]

        def sb(name, shape, dt=F32):
            n = 4
            for d in shape[1:]:
                n *= d
            here = spot[0]
            spot[0] += (n + 31) // 32 * 32
            return at(name, here, shape, dt)

        ident = sb("ident", [P, P])
        ones = sb("ones", [P, P])
        tri = sb("tri", [P, P])
        vec_rows, conv_rows = hn[0:68, 0, 0:P], hn[0:CONV_K, 1:3, :].rearrange("p k n -> p (k n)")
        iota_i = hn[:, 3, 0:P].bitcast(I32)
        iota_f = sb("iota_f", [P, P])
        vec = sb("vec", [P, 68])
        conv_w = sb("conv_w", [P, KC, CONV_K])
        inv_cnt = sb("inv_cnt", [P, NG, 16])
        std = sb("std", [P, SEQ])
        rstd = sb("rstd", [P, SEQ])
        sinks = sb("sinks", [P, NH])
        router = sb("router", [P, KD, NE])
        small = sb("small", [P, 352])
        jobs_i = sb("jobs_i", [1, 3, NJ], I32)
        eps = sb("eps", [P, 1])

        taken = {"b": 0, "c": 0}

        def part(where, *dims):
            n = 1
            for d in dims:
                n *= d
            first = taken[where]
            taken[where] += n
            assert taken[where] * 4 <= (AREA_B if where == "b" else AREA_C), (where, taken)
            names = "abcd"[:len(dims)]
            return area[where][:, first:first + n].rearrange(
                f"p ({' '.join(names)}) -> p {' '.join(names)}", **{c: d for c, d in zip(names, dims)})

        PADC, PADP = CONV_K - 1, 16
        glu = part("b", KC, PADC + SEQ)
        conv = part("b", KC, SEQ)
        conv_b2 = part("b", SEQ)
        mix = part("b", KD, SEQ)
        pool_t = part("b", 2, PADP + SEQ)
        pool_in = part("c", NG, PADP + SEQ)
        conv_p, products = sq[:, 4:6, :], sq[:, 6:8, :]
        sig = part("c", 2, SEQ)
        pool_w = part("c", NG, P)
        taken["c"] = 0
        ff_sg = part("c", 2, SEQ)
        ff_high = at("ff_high", KEEP_AT + 4 * K8 + 2 * SEQ * 4, [P, 2, SEQ], F32R)
        ff_low = at("ff_low", KEEP_AT + 4 * K8 + 4 * SEQ * 4, [P, 2, SEQ], F32R)
        ff_prod = at("ff_prod", KEEP_AT + 4 * K8 + 6 * SEQ * 4, [P, 2, SEQ])
        taken["c"] = 0
        taken["b"] = 0
        vN = part("c", NB, NKV * HD)
        b_v = part("c", NKV * HD)[0:1, :]
        kT = part("b", NKV, SEQ)
        probsT = part("b", 4, 3 * P)
        mask = part("b", 3 * P)
        part("b", P)
        oT = part("b", KD, SEQ)
        probs = sq[:, 0:6, :].rearrange("p k n -> p (k n)").rearrange("p (h n) -> p h n", h=4)
        qT = nat[:, :, :].rearrange("p b (k n) -> p (b k) n", n=SEQ)
        mx = small[:, 0:2 * NH]
        negm = small[:, 32:32 + 2 * NH]
        rsum = small[:, 64:64 + 2 * NH]
        esink = small[:, 96:96 + 2 * NH]
        den = small[:, 128:128 + 2 * NH]
        rden = small[:, 160:160 + 2 * NH]
        taken["c"] = 0
        ys_high = at("ys_high", KEEP_AT + 4 * K8, [P, D], F32R)
        ys_low = at("ys_low", KEEP_AT + 2 * K8 + K8 // 2, [P, D], F32R)
        jt = part("c", D).rearrange("p (a n) -> p a n", a=8)[:, 0:4, 0:NJ * NE].rearrange("p a (j e) -> p a j e", e=NE)
        sel = part("c", NB, P)
        selT = at("selT", KEEP_AT + 4 * K8 + (D + NB * P) * 4, [P, NB * P], F32R)
        res = sq[:, :, :].rearrange("p k n -> p (k n)").rearrange("p (b d) -> p b d", b=NB)
        logitsT = std[0:NE, :]
        logits = small[:, 192:208].rearrange("p (b e) -> p b e", b=NB)
        less = small[:, 208:224].rearrange("p (b e) -> p b e", b=NB)
        place = small[:, 224:240].rearrange("p (b e) -> p b e", b=NB)
        first = small[:, 240:256].rearrange("p (b e) -> p b e", b=NB)
        second = small[:, 256:272].rearrange("p (b e) -> p b e", b=NB)
        chosen = small[:, 272:288].rearrange("p (b e) -> p b e", b=NB)
        gates = small[:, 288:304].rearrange("p (b e) -> p b e", b=NB)
        slots = small[:, 304:320].rearrange("p (b e) -> p b e", b=NB)
        iota_e = small[:, 320:336].rearrange("p (b e) -> p b e", b=NB)
        top1, top2, arg = small[:, 336:338], small[:, 338:340], small[:, 340:342]
        ratio, share1, share2 = small[:, 342:344], small[:, 344:346], small[:, 346:348]
        ssq = small[:, 348:350]
        frstd = small[:, 350:352]
        je = sb("job_rows", [P, 8, 16])
        tN = sq[:, :, :].rearrange("p k n -> p (k n)").rearrange("p (b d) -> p b d", b=NB)

        VEC = {}
        at = 0
        for name, ap, n in (("norm1", e_norm1, 8), ("conv_b", e_conv_b, 4), ("ln_g", e_ln_g, 4),
                            ("ln_b", e_ln_b, 4), ("pool_scale", e_pool_scale, 4), ("norm2", e_norm2, 8),
                            ("onorm1", o_norm1, 8), ("b_qk", o_b_qkv, 12), ("b_o", o_b_o, 8),
                            ("onorm2", o_norm2, 8)):
            VEC[name] = (at, n, ap)
            at += n

        def col(name, k):
            return vec[:, VEC[name][0] + k:VEC[name][0] + k + 1]

        eps_ready = sem("eps_ready")
        x_loaded = sem("x_loaded")
        small_loaded = sem("small_loaded")
        bv_loaded = sem("bv_loaded")
        fnorm_loaded = sem("fnorm_loaded")
        win_loaded = [sem(f"win_loaded{c}") for c in range(KC + 1)]
        wout_loaded = [sem(f"wout_loaded{c}") for c in range(2)]
        ff_loaded = [sem(f"ff_loaded{q}") for q in range(3)]
        qkv_loaded = sem("qkv_loaded")
        wo_loaded = sem("wo_loaded")
        raw_loaded = [sem(f"raw_loaded{s}") for s in range(RAW)]
        const_step = sem("const_step")
        consts = sem("consts")
        pads = sem("pads")
        xT_done = sem("xT_done")
        vecT_done = sem("vecT_done")
        vec_ready = sem("vec_ready")
        res_ready = [sem(f"res_ready{n}") for n in range(4)]
        sq_ready = [sem(f"sq_ready{n}") for n in range(4)]
        pair_ready = [sem(f"pair_ready{n}") for n in range(4)]
        ss_done = [sem(f"ss_done{n}") for n in range(4)]
        std_ready = [sem(f"std_ready{n}") for n in range(4)]
        rstd_ready = [sem(f"rstd_ready{n}") for n in range(4)]
        hn_ready = [sem(f"hn_ready{n}") for n in range(4)]
        u_done = sem("u_done")
        sig_ready = sem("sig_ready")
        glu_ready = sem("glu_ready")
        b_done = sem("b_done")
        b_ready = sem("b_ready")
        pool_step = sem("pool_step")
        pool_ready = sem("pool_ready")
        pmap_done = sem("pmap_done")
        pmix_ready = sem("pmix_ready")
        conv_step = sem("conv_step")
        conv_ready = sem("conv_ready")
        product_ready = sem("product_ready")
        product_added = sem("product_added")
        mean_done = sem("mean_done")
        cent_ready = sem("cent_ready")
        lsq_ready = sem("lsq_ready")
        var_done = sem("var_done")
        lstd_ready = sem("lstd_ready")
        lrstd_ready = sem("lrstd_ready")
        ln_ready = sem("ln_ready")
        cmix_ready = sem("cmix_ready")
        wout_done = sem("wout_done")
        hn_high_ready = sem("hn_high_ready")
        hn_low_ready = sem("hn_low_ready")
        ff_w_high = sem("ff_w_high")
        ff_w_low = sem("ff_w_low")
        ff_cleared = sem("ff_cleared")
        ff_h1_done = sem("ff_h1_done")
        ff_h3_done = sem("ff_h3_done")
        ff_sg_ready = sem("ff_sg_ready")
        ff_prod_ready = sem("ff_prod_ready")
        ff_high_ready = sem("ff_high_ready")
        ff_low_ready = sem("ff_low_ready")
        ff_down_done = sem("ff_down_done")
        k_done = sem("k_done")
        v_done = sem("v_done")
        q_done = sem("q_done")
        k_half = sem("k_half")
        k_ready = sem("k_ready")
        v_ready = sem("v_ready")
        q_ready = sem("q_ready")
        s_done = sem("s_done")
        s_masked = sem("s_masked")
        neg_ready = sem("neg_ready")
        e_ready = sem("e_ready")
        den_step = sem("den_step")
        p_ready = sem("p_ready")
        pT_done = sem("pT_done")
        pT_dve = sem("pT_dve")
        pT_act = sem("pT_act")
        o_done = sem("o_done")
        o_ready = sem("o_ready")
        wo_done = sem("wo_done")
        logitT_done = sem("logitT_done")
        logitT_ready = sem("logitT_ready")
        logit_done = sem("logit_done")
        n_jobs_ready = sem("n_jobs_ready")
        tN_done = sem("tN_done")
        tN_ready = sem("tN_ready")
        acc_done = sem("acc_done")
        acc_ready = sem("acc_ready")
        route = sem("route")
        top_ready = sem("top_ready")
        ratio_ready = sem("ratio_ready")
        chosen_ready = sem("chosen_ready")
        place_done = sem("place_done")
        jobs_ready = sem("jobs_ready")
        sel_ready = sem("sel_ready")
        gathered = sem("gathered")
        high_ready = sem("high_ready")
        low_ready = sem("low_ready")
        unit_done = sem("unit_done")
        x_high_ready = sem("x_high_ready")
        x_low_ready = sem("x_low_ready")
        selT_done = sem("selT_done")
        selT_ready = sem("selT_ready")
        gate_ready = sem("gate_ready")
        prod_ready = sem("prod_ready")
        turned = sem("turned")
        h_high_ready = sem("h_high_ready")
        h_low_ready = sem("h_low_ready")
        ys_high_ready = sem("ys_high_ready")
        ys_low_ready = sem("ys_low_ready")
        back_done = sem("back_done")
        back_added = sem("back_added")
        ssq_ready = sem("ssq_ready")
        fstd_ready = sem("fstd_ready")
        frstd_ready = sem("frstd_ready")
        final_ready = sem("final_ready")
        stored = sem("stored")

        SMALL_LOADS = [(hn[at:at + n, 0, 0:P], ap[0].rearrange("(r n) -> r n", n=P)[0:n])
                       for at, n, ap in VEC.values()]
        SMALL_LOADS += [(conv_rows, e_conv_w[0]), (pool_w, e_pool_w[0].rearrange("g c d -> c g d")),
                        (sinks[:, :], o_sinks[0:1, :].broadcast_to([P, NH])),
                        (router[:, :, :], o_router[0].rearrange("(k p) e -> p k e", p=P))]
        N_SMALL = len(SMALL_LOADS)

        def load_small(eng, loads):
            for dst, src in loads:
                eng.dma_start(dst, src).then_inc(small_loaded, 16)

        N_CONST = 6
        HEAD = 1

        block = ctx.enter_context(nc.Block())

        LAST_W1 = [stream.index(("up", g, 1)) for g in range(GROUPS)]
        LAST_UP = [stream.index(("up", g, 3)) for g in range(GROUPS)]
        POOL_ORDER = list(range(NG))[::-1]
        POOL_MAP = [(6 + g % 2, slice(g // 2 * SEQ, (g // 2 + 1) * SEQ)) for g in range(NG)]
        OUT_BANKS, MEAN, VAR = (0, 1, 4, 5), 2, 3
        POOL_TAPS = 10
        TAKE_H = [min(n + 5, UNITS - 1) for n in LAST_UP]

        @block.sync
        def _(sp):
            sp.dma_start(nat[:, :, :], x[0].rearrange("(b p) d -> p b d", p=P)).then_inc(x_loaded, 16)
            load_small(sp, SMALL_LOADS[::2])
            w_in_d = e_w_in[0].rearrange("(k p) n -> p k n", p=P)
            for c in range(KC):
                for part_at in (c * P, D_CONV + c * P):
                    sp.dma_start(w_in[:, :, part_at:part_at + P],
                                 w_in_d[:, :, part_at:part_at + P]).then_inc(win_loaded[c], 16)
            sp.dma_start(w_in[:, :, 2 * D_CONV:], w_in_d[:, :, 2 * D_CONV:]).then_inc(win_loaded[KC], 16)
            w_out_d = e_w_out[0].rearrange("(k p) n -> p k n", p=P)
            for c in range(2):
                k0 = (1 - c) * 4
                sp.dma_start(w_out[:, k0:k0 + 4, :], w_out_d[:, k0:k0 + 4, :]).then_inc(wout_loaded[c], 16)

            ff_d = [w[0].rearrange("(k p) (g n) -> g p k n", p=P, n=2 * P) for w in (e_ff_w1, e_ff_w3)]
            ff_d.append(e_ff_w2[0].rearrange("(g f p) n -> g p f n", p=P, f=2))

            def load_ff(g, q):
                src = ff_d[q][g] if isinstance(g, int) else ff_d[q][bass.ds(g, 1)].rearrange("g p a n -> p (g a) n")
                sp.dma_start(raw[:, FF_RAW[q], :].rearrange("p (a n) -> p a n", a=src.shape[1]), src
                             ).then_inc(ff_loaded[q], 16)

            for q in range(3):
                load_ff(0, q)
            sp.wait_ge(b_done, NG)
            sp.dma_start(w_qkv[:, :, :], o_w_qkv[0].rearrange("(k p) n -> p k n", p=P)).then_inc(qkv_loaded, 16)
            with sp.Fori(0, FFG - 1) as g:
                for q in range(3):
                    sp.wait_ge(ff_w_low, 3 * g + q + 1)
                    load_ff(g + 1, q)
            sp.dma_start(w_o[:, :, :], o_w_o[0].rearrange("(k p) n -> p k n", p=P)).then_inc(wo_loaded, 16)

            up_d = [w[0].rearrange("e (k p) n -> e p k n", p=P) for w in (o_exp_w1, o_exp_w3)]
            down_d = o_exp_w2[0].rearrange("e (f p) n -> e p f n", p=P)

            def load_unit(e, i):
                kind, g, n = stream[i]
                s = raw_slot[i]
                if kind == "up":
                    src = up_d[n // 2][bass.ds(e, 1), :, (n % 2) * 4:(n % 2) * 4 + 4, g * GF * P:(g + 1) * GF * P]
                else:
                    src = down_d[bass.ds(e, 1), :, g * GF + 2 * n:g * GF + 2 * n + 2, :]
                a = src.shape[2]
                sp.dma_start(raw[:, s, :].rearrange("p (a n) -> p a n", a=a),
                             src.rearrange("e p a n -> p (e a) n")).then_inc(raw_loaded[s], 16)

            sp.wait_ge(ff_w_low, 3 * FFG)
            for i in range(UNITS):
                if i == 4:
                    sp.wait_ge(q_done, KD)
                if i == 10:
                    sp.wait_ge(wo_done, 4)
                if i >= RAW:
                    sp.wait_ge(low_ready, i - RAW + 1)
                load_unit(0, i)
            sp.wait_ge(jobs_ready, 1)
            n_more = sp.value_load(jobs_i[0:1, 2, 1:2], min_val=NE - 1, max_val=MAX_JOBS - 1)
            with sp.Fori(0, n_more) as j:
                e = sp.value_load(jobs_i[0:1, 0, bass.ds(j + 1, 1)], min_val=0, max_val=NE - 1)
                for i in range(UNITS):
                    sp.wait_ge(low_ready, UNITS * j + (UNITS + i - RAW + 1))
                    load_unit(e, i)
            sp.wait_ge(unit_done, UNITS * n_more + (SPLIT + LAST_UP[-1] + 1))
            sp.dma_start(fnorm[:, :], final_norm.rearrange("(a d) -> a d", a=1).broadcast_to([P, D])
                         ).then_inc(fnorm_loaded, 16)
            for n in range(2 * NB):
                b, half = divmod(n, 2)
                sp.wait_ge(final_ready, n + 1)
                cols = slice(half * D // 2, (half + 1) * D // 2)
                sp.dma_start(out[0, b * P:(b + 1) * P, cols], res[:, b, cols]).then_inc(stored, 16)
            sp.wait_ge(stored, 16 * 2 * NB)

        @block.gpsimd
        def _(pool):
            steps = [0]

            def then(ins):
                steps[0] += 1
                ins.then_inc(const_step, 1)
                pool.wait_ge(const_step, steps[0])

            then(pool.memset(ident[:, :], 0.0))
            pool.affine_select(out=ident[:, :], in_=ident[:, :], compare_op=ALU.not_equal, fill=1.0, base=0,
                               pattern=[[-1, P]], channel_multiplier=1).then_inc(consts, 1)
            pool.memset(ones[:, :], 1.0).then_inc(consts, 1)
            for t in (glu[:, :, 0:PADC], pool_in[:, :, 0:PADP]):
                pool.memset(t, 0.0).then_inc(pads, 1)
            then(pool.memset(pool_t[:, :, 0:PADP], 0.0))
            then(pool.memset(tri[:, :], 1.0))
            pool.affine_select(out=tri[:, :], in_=tri[:, :], compare_op=ALU.is_gt, fill=0.0, base=0,
                               pattern=[[1, P]], channel_multiplier=-1).then_inc(consts, 1)
            then(pool.iota(iota_i, pattern=[[1, P]], base=0, channel_multiplier=0))
            pool.tensor_copy(iota_f[:, :], iota_i).then_inc(consts, 1)
            pool.wait_ge(consts, 4)
            for g in range(NG):
                w = float(2 << g)
                then(pool.tensor_scalar(inv_cnt[:, g, :], iota_f[:, 0:16], 1.0, w, ALU.add, ALU.min))
            pool.tensor_copy(iota_e, iota_f[:, 0:NE].unsqueeze(1).broadcast_to([P, NB, NE])).then_inc(consts, 1)
            pool.nop().then_inc(consts, 1)

            psteps = [0]

            def link(ins):
                psteps[0] += 1
                ins.then_inc(pool_step, 1)
                pool.wait_ge(pool_step, psteps[0])

            for c in range(2):
                for j in range(1, POOL_TAPS):
                    pool.wait_ge(product_ready, POOL_TAPS * c + j + 1)
                    ins = pool.tensor_tensor(conv_p[:, c, :], conv_p[:, c, :], products[:, j % 2, :], ALU.add)
                    ins.then_inc(product_added, 1)
                    pool.wait_ge(product_added, (POOL_TAPS - 1) * c + j)
            pool.wait_ge(vec_ready, 3)
            for n, g in enumerate(POOL_ORDER):
                pool.wait_ge(b_ready, n + 1)
                cur = pool_in[:, g, :]
                for s in range(g + 1):
                    nxt = pool_t[:, s % 2, :]
                    lag = 1 << s
                    link(pool.tensor_tensor(nxt[:, PADP:], cur[:, PADP:], cur[:, PADP - lag:PADP + SEQ - lag],
                                            ALU.add))
                    cur = nxt
                link(pool.tensor_tensor(cur[:, PADP:PADP + 16], cur[:, PADP:PADP + 16], inv_cnt[:, g, :], ALU.mult))
                link(pool.tensor_scalar(cur[:, PADP + 16:], cur[:, PADP + 16:], 1.0 / (2 << g), None, ALU.mult))
                ins = pool.tensor_tensor(pool_in[:, g, PADP:], cur[:, PADP:], pool_in[:, g, PADP:], ALU.subtract)
                link(ins)
                pool.nop().then_inc(pool_ready, 1)

            pool.wait_ge(ff_down_done, HEAD + 4 * FFG)
            pool.dma_start(b_v, o_b_qkv[0:1, D_QKV - NKV * HD:]).then_inc(bv_loaded, 16)
            pool.memset(mask, 0.0).then_inc(const_step, 1)
            base = steps[0] + 1
            pool.wait_ge(const_step, base)
            for n, (mult, step) in enumerate(((1, -1), (-1, 1), (1, -1))):
                off = -1 if n == 1 else 0
                pool.affine_select(out=mask[:, n * P:(n + 1) * P], in_=mask[:, n * P:(n + 1) * P],
                                   compare_op=ALU.is_ge, fill=NEG, base=off, pattern=[[step, P]],
                                   channel_multiplier=mult).then_inc(const_step, 1)


        MASK_STEPS = 1 + 2 + 1 + NG + 4

        @block.tensor
        def _(pe):
            def sum_squares(n, bank):
                for k in range(KD):
                    if k % 2 == 0:
                        pe.wait_ge(sq_ready[n], k // 2 + 1)
                    mm = pe.matmul(PS[:, bank, 0:SEQ], ones[:, :], sq[:, k, :], start=(k == 0), stop=(k == KD - 1))
                mm.then_inc(ss_done[n], 1)

            def sum_pair(n, bank, i):
                pe.wait_ge(pair_ready[n], i + 1)
                mm = pe.matmul(PS[:, bank, 0:SEQ], ones[:, :], sq[:, 2 * i, :], start=(i == 0), stop=(i == KD // 2 - 1))
                if i == KD // 2 - 1:
                    mm.then_inc(ss_done[n], 1)

            for s in (ff_down_done, back_done):
                pe.sem_inc(s, HEAD)
            pe.sem_inc(unit_done, SPLIT)

            pe.wait_ge(consts, 2)
            pe.wait_ge(x_loaded, 16)
            for i in range(4):
                for kk in range(2):
                    for b in range(NB):
                        k = 2 * i + kk
                        mm = pe.transpose(PS[:, i, (kk * 2 + b) * P:(kk * 2 + b + 1) * P],
                                          nat[:, b, k * P:(k + 1) * P], ident[:, :])
                mm.then_inc(xT_done, 1)
            pe.wait_ge(small_loaded, 16 * N_SMALL)
            pe.transpose(PS[:, 4, 0:68], vec_rows, ident[0:68, 0:68])
            for c in range(KC):
                mm = pe.transpose(PS[:, 4, 128 + 32 * c:128 + 32 * c + CONV_K], conv_rows[:, c * P:(c + 1) * P],
                                  ident[0:CONV_K, 0:CONV_K])
            mm.then_inc(vecT_done, 1)
            sum_squares(0, 7)

            for c in range(KC):
                pe.wait_ge(win_loaded[c], 32)
                for i in range(2):
                    at = i * D_CONV + c * P
                    for k in range(KD):
                        if c == 0 and i == 0:
                            pe.wait_ge(hn_ready[0], k + 1)
                        mm = pe.matmul(PS[:, c, i * SEQ:(i + 1) * SEQ], w_in[:, k, at:at + P], hn[:, k, :],
                                       start=(k == 0), stop=(k == KD - 1))
                mm.then_inc(u_done, 1)
            pe.wait_ge(win_loaded[KC], 16)
            for g in POOL_ORDER:
                at = 2 * D_CONV + g * P
                for k in range(KD):
                    mm = pe.matmul(PS[:, 4 + g, 0:SEQ], w_in[:, k, at:at + P], hn[:, k, :],
                                   start=(k == 0), stop=(k == KD - 1))
                mm.then_inc(b_done, 1)
            def pool_map(n):
                g = POOL_ORDER[n]
                pe.wait_ge(pool_ready, n + 1)
                pe.matmul(PS[:, *POOL_MAP[g]], pool_w[:, g, :], pool_in[:, g, PADP:],
                          start=True, stop=True).then_inc(pmap_done, 1)

            def out_terms(m, ks, first=False, last=False):
                for k in ks:
                    mm = pe.matmul(PS[:, OUT_BANKS[m // 2], (m % 2) * SEQ:(m % 2 + 1) * SEQ],
                                   w_out[:, k, m * P:(m + 1) * P], mix[:, k, :], start=first and m % 2 == 0,
                                   stop=last, skip_group_check=True)
                return mm

            pool_map(0)
            for n, g in enumerate(POOL_ORDER):
                if n + 1 < NG:
                    pool_map(n + 1)
                if n == 0:
                    pe.wait_ge(wout_loaded[0], 16)
                    pe.wait_ge(glu_ready, 2)
                    pe.wait_ge(b_ready, NG)
                if n == NG - 2:
                    pe.wait_ge(glu_ready, KC)
                    for c in range(KC):
                        pe.wait_ge(conv_ready, c + 1)
                        mm = pe.matmul(PS[:, MEAN, 0:SEQ], ones[:, :], conv[:, c, :], start=(c == 0),
                                       stop=(c == KC - 1))
                    mm.then_inc(mean_done, 1)
                if n == NG - 1:
                    for c in range(KC):
                        pe.wait_ge(lsq_ready, c + 1)
                        mm = pe.matmul(PS[:, VAR, 0:SEQ], ones[:, :], sq[:, c, :], start=(c == 0),
                                       stop=(c == KC - 1))
                    mm.then_inc(var_done, 1)
                pe.wait_ge(pmix_ready, n + 1)
                for m in range(KD):
                    out_terms(m, [KC + g], first=(n == 0))
            pe.wait_ge(wout_loaded[1], 16)
            for m in range(KD):
                for k in range(KC):
                    if m == 0:
                        pe.wait_ge(cmix_ready, k + 1)
                    mm = out_terms(m, [k], last=(k == KC - 1))
                if m % 2:
                    mm.then_inc(wout_done, 1)
                    if m > 1:
                        sum_pair(1, 7, m // 2 - 1)
            sum_pair(1, 7, KD // 2 - 1)

            pe.wait_ge(ff_cleared, 4)
            with pe.Fori(0, FFG) as g:
                for q in range(2):
                    pe.wait_ge(ff_w_low, 3 * g + q + 1)
                    for f in range(2):
                        if q == 0:
                            pe.wait_ge(ff_prod_ready, HEAD + 2 * g)
                        dst = PS[:, 4 + 2 * q + f, 0:SEQ]
                        for n, (wt, v, v_ready) in enumerate(((high, hn_high, hn_high_ready),
                                                              (low, hn_high, hn_high_ready),
                                                              (high, hn_low, hn_low_ready))):
                            for k in range(KD):
                                if q == 0 and f == 0 and n != 1:
                                    pe.wait_ge(v_ready, k + 1)
                                w = slice(k * 2 * P + f * P, k * 2 * P + (f + 1) * P)
                                mm = pe.matmul(dst, wt[:, q, w], v[:, k, :], start=(n == 0 and k == 0),
                                               stop=(n == 2 and k == KD - 1))
                        mm.then_inc((ff_h1_done, ff_h3_done)[q], 1)
                pe.wait_ge(ff_w_low, 3 * g + 3)
                for f in range(2):
                    pe.wait_ge(ff_low_ready, 2 * g + f + 1)
                    for m in range(KD):
                        w = slice(f * D + m * P, f * D + (m + 1) * P)
                        dst = PS[:, m // 2, (m % 2) * SEQ:(m % 2 + 1) * SEQ]
                        for wt, v in ((high, ff_high), (high, ff_low), (low, ff_high)):
                            mm = pe.matmul(dst, wt[:, 2, w], v[:, f, :], start=False, stop=True,
                                           skip_group_check=True)
                        if f == 1 and m % 2:
                            mm.then_inc(ff_down_done, 1)
            sum_squares(2, 7)

            pe.wait_ge(qkv_loaded, 16)
            for m in range(2):
                at = D + m * P
                for k in range(KD):
                    if m == 0:
                        pe.wait_ge(hn_ready[2], k + 1)
                    mm = pe.matmul(PS[:, m, 0:SEQ], w_qkv[:, k, at:at + P], hn[:, k, :],
                                   start=(k == 0), stop=(k == KD - 1))
                mm.then_inc(k_done, 1)
            pe.wait_ge(bv_loaded, 16)
            for b in range(NB):
                for k in range(KD):
                    pe.matmul(PS[:, 2 + b, 0:NKV * HD], hn[:, k, b * P:(b + 1) * P], w_qkv[:, k, D + 2 * P:],
                              start=(k == 0), stop=False)
                pe.matmul(PS[:, 2 + b, 0:NKV * HD], ones[0:1, :], b_v, start=False, stop=True
                          ).then_inc(v_done, 1)

            def queries(m):
                if m >= 2:
                    pe.wait_ge(q_ready, m - 1)
                for k in range(KD):
                    mm = pe.matmul(PS[:, 4 + m % 2, 0:SEQ], w_qkv[:, k, m * P:(m + 1) * P], hn[:, k, :],
                                   start=(k == 0), stop=(k == KD - 1))
                mm.then_inc(q_done, 1)

            def scores(m):
                pe.wait_ge(q_ready, m + 1)
                pe.wait_ge(k_ready, NKV)
                for i in range(2):
                    h, j = 2 * m + i, (2 * m + i) // (NH // NKV)
                    if h >= 2:
                        pe.wait_ge(s_masked, h - 1)
                    r0 = HD * i
                    pe.matmul(PS[:, 6 + i, 0:P], qT[r0:r0 + HD, m, 0:P], kT[r0:r0 + HD, j, 0:P],
                              start=True, stop=True)
                    pe.matmul(PS[:, 6 + i, P:3 * P], qT[r0:r0 + HD, m, P:2 * P], kT[r0:r0 + HD, j, 0:2 * P],
                              start=True, stop=True).then_inc(s_done, 1)

            def turn_probs(m):
                pe.wait_ge(p_ready, m + 1)
                if m == 0:
                    pe.wait_ge(k_ready, NKV)
                else:
                    pe.wait_ge(pT_dve, m)
                    pe.wait_ge(pT_act, m)
                for i in range(2):
                    h = 2 * m + i
                    for n in range(3):
                        mm = pe.transpose(PS[:, i, n * P:(n + 1) * P], probs[:, h % 4, n * P:(n + 1) * P],
                                          ident[:, :])
                    mm.then_inc(pT_done, 1)

            def values(m):
                if m >= 2:
                    pe.wait_ge(o_ready, m - 1)
                else:
                    pe.wait_ge(v_ready, NB)
                pe.wait_ge(pT_dve, m + 1)
                pe.wait_ge(pT_act, m + 1)
                for i in range(2):
                    h = 2 * m + i
                    j = h // (NH // NKV)
                    dst = PS[HD * i:HD * (i + 1), 2 + m % 2, :]
                    v0, v1 = (vN[:, b, j * HD:(j + 1) * HD] for b in range(NB))
                    pe.matmul(dst[:, 0:P], v0, probsT[:, h % 4, 0:P], start=True, stop=True)
                    pe.matmul(dst[:, P:2 * P], v0, probsT[:, h % 4, P:2 * P], start=True, stop=False)
                    mm = pe.matmul(dst[:, P:2 * P], v1, probsT[:, h % 4, 2 * P:3 * P], start=False, stop=True)
                mm.then_inc(o_done, 1)

            def project(m, ks):
                for k in ks:
                    pe.wait_ge(o_ready, k + 1)
                    mm = pe.matmul(PS[:, 4 + m // 2, (m % 2) * SEQ:(m % 2 + 1) * SEQ], w_o[:, k, m * P:(m + 1) * P],
                                   oT[:, k, :], start=(k == 0 and m % 2 == 0), stop=(k == KD - 1),
                                   skip_group_check=True)
                return mm

            EARLY = {KD: (0, 1, 2), KD + 1: (3, 4), KD + 2: (5,)}
            for s in range(KD + 3):
                if s < KD:
                    queries(s)
                if 0 <= s - 1 < KD:
                    scores(s - 1)
                if s == KD:
                    pe.wait_ge(wo_loaded, 16)
                    pe.wait_ge(q_ready, KD)
                for k in EARLY.get(s, ()):
                    for m in range(KD // 2):
                        project(m, [k])
                if 0 <= s - 2 < KD:
                    turn_probs(s - 2)
                if 0 <= s - 3 < KD:
                    values(s - 3)

            for m in range(KD):
                if m == KD // 2:
                    pe.wait_ge(s_masked, NH)
                mm = project(m, range(6, KD) if m < KD // 2 else range(KD))
                if m % 2:
                    mm.then_inc(wo_done, 1)
                    if m > 1:
                        sum_pair(3, 0, m // 2 - 1)
            sum_pair(3, 0, KD // 2 - 1)

            for i in range(4):
                b, half = divmod(i, 2)
                if i >= 2:
                    pe.wait_ge(acc_ready, i - 1)
                else:
                    pe.wait_ge(res_ready[3], 4)
                for kk in range(4):
                    mm = pe.transpose(PS[:, 6 + i % 2, kk * P:(kk + 1) * P],
                                      hT[:, half * 4 + kk, b * P:(b + 1) * P], ident[:, :])
                mm.then_inc(acc_done, 1)
            for k in range(KD):
                pe.wait_ge(hn_ready[3], k + 1)
                mm = pe.matmul(PS[0:NE, 1, 128:128 + SEQ], router[:, k, :], hn[:, k, :],
                               start=(k == 0), stop=(k == KD - 1))
            mm.then_inc(logitT_done, 1)
            pe.wait_ge(logitT_ready, 1)
            for b in range(NB):
                mm = pe.transpose(PS[:, 1, b * NE:(b + 1) * NE], logitsT[:, b * P:(b + 1) * P], ident[0:NE, 0:NE])
            mm.then_inc(logit_done, 1)
            for i in range(4):
                b, half = divmod(i, 2)
                for kk in range(4):
                    mm = pe.transpose(PS[:, 2 + i, kk * P:(kk + 1) * P],
                                      hn[:, half * 4 + kk, b * P:(b + 1) * P], ident[:, :])
                mm.then_inc(tN_done, 1)
            pe.wait_ge(chosen_ready, 1)
            pe.matmul(PS[:, 1, 32:32 + NE], tri[:, :], chosen[:, 0, :], start=True, stop=True)
            pe.matmul(PS[:, 1, 32 + NE:32 + 2 * NE], ones[:, :], chosen[:, 0, :], start=True, stop=False)
            pe.matmul(PS[:, 1, 32 + NE:32 + 2 * NE], tri[:, :], chosen[:, 1, :], start=False, stop=True)
            pe.matmul(PS[:, 1, 64:64 + NE], ones[:, :], chosen[:, 0, :], start=True, stop=False)
            pe.matmul(PS[:, 1, 64:64 + NE], ones[:, :], chosen[:, 1, :], start=False, stop=True
                      ).then_inc(place_done, 1)

            H1, Y, T, SPARE = (0, 2), 4, 6, 7

            def gather(j, half):
                pe.wait_ge(sel_ready, j + 1)
                for m in range(4 * half, 4 * half + 4):
                    for b in range(NB):
                        mm = pe.matmul(PS[:, 2 + m // 4, (m % 4) * P:(m % 4 + 1) * P],
                                       tN[:, b, m * P:(m + 1) * P], sel[:, b, :],
                                       start=(b == 0), stop=(b == NB - 1))
                mm.then_inc(gathered, 1)

            def turn_sel(j):
                pe.wait_ge(x_high_ready, 2 * j + 1)
                pe.wait_ge(x_low_ready, 2 * j + 1)
                for b in range(NB):
                    mm = pe.transpose(PS[:, 2, b * P:(b + 1) * P], sel[:, b, :], ident[:, :])
                mm.then_inc(selT_done, 1)

            def turn_hidden(j, g):
                pe.wait_ge(prod_ready, HEAD + GROUPS * j + g + 1)
                if g:
                    pe.wait_ge(h_low_ready, GROUPS * j + g)
                else:
                    pe.wait_ge(back_added, HEAD + 4 * j)
                for f in range(GF):
                    mm = pe.transpose(PS[:, T, f * P:(f + 1) * P], prod_h[:, f * P:(f + 1) * P], ident[:, :])
                mm.then_inc(turned, 1)

            def unit(j, i, between=None):
                kind, g, n = stream[i]
                s = i % SPLIT
                if kind == "up" and n == 0:
                    if g == 0:
                        pe.wait_ge(x_low_ready, 2 * j + 1)
                        pe.wait_ge(prod_ready, HEAD + GROUPS * j)
                    elif g == 1:
                        pe.wait_ge(selT_ready, j + 1)
                    else:
                        pe.wait_ge(prod_ready, HEAD + GROUPS * j + g - 1)
                if (kind, g, n) == ("up", 0, 1):
                    pe.wait_ge(x_low_ready, 2 * j + 2)
                if kind == "down" and n == 0:
                    if g == 0:
                        pe.wait_ge(back_added, HEAD + 4 * j)
                    pe.wait_ge(h_low_ready, GROUPS * j + g + 1)
                pe.wait_ge(low_ready, UNITS * j + i + 1)
                for a in range(4):
                    if kind == "up":
                        k = (n % 2) * 4 + a
                        dst = PS[:, H1[g % 2] + n // 2, :]
                        w = slice(a * GF * P, (a + 1) * GF * P)
                        first, last = k == 0, k == KD - 1
                        own_high, own_low = x_high[:, k, :], x_low[:, k, :]
                    else:
                        f = 2 * n + a // 2
                        dst = PS[:, Y + a % 2, :]
                        w = slice(a * 512, (a + 1) * 512)
                        first, last = g == 0 and f == 0, g == GROUPS - 1 and f == GF - 1
                        own_high, own_low = h_high[:, f, :], h_low[:, f, :]
                    pe.matmul(dst, own_high, high[:, s, w], start=first, stop=False)
                    pe.matmul(dst, own_high, low[:, s, w], start=False, stop=False)
                    mm = pe.matmul(dst, own_low, high[:, s, w], start=False, stop=last)
                    if a == 1 and between:
                        between()
                mm.then_inc(unit_done, 1)

            def way_back(j):
                for n, bank in enumerate((T, SPARE, Y, Y + 1)):
                    b, half = divmod(n, 2)
                    if b == 0:
                        pe.wait_ge(ys_low_ready, 2 * j + half + 1)
                    to, cols = selT[:, b * P:(b + 1) * P], slice(half * 512, (half + 1) * 512)
                    pe.matmul(PS[:, bank, :], to, ys_high[:, cols], start=True, stop=False)
                    pe.matmul(PS[:, bank, :], to, ys_low[:, cols], start=False, stop=True).then_inc(back_done, 1)

            pe.wait_ge(tN_ready, 4)
            pe.wait_ge(acc_ready, 4)
            for half in range(2):
                gather(0, half)
            turn_sel(0)
            pe.wait_ge(n_jobs_ready, 1)
            n_more = pe.value_load(jobs_i[0:1, 2, 1:2], min_val=NE - 1, max_val=MAX_JOBS - 1)

            def job(j, last):
                for i in range(UNITS):
                    if i == UNITS - 2 and not last:
                        gather(j + 1, 0)
                    if i == LAST_UP[-1] + 2:
                        unit(j, i, lambda: turn_hidden(j, GROUPS - 1))
                    else:
                        unit(j, i)
                        if i - 2 in LAST_UP:
                            turn_hidden(j, LAST_UP.index(i - 2))
                if not last:
                    gather(j + 1, 1)
                way_back(j)
                if not last:
                    turn_sel(j + 1)

            with pe.Fori(0, n_more) as j:
                job(j, False)
            job(n_more, True)

        @block.scalar
        def _(act):
            def squares(n):
                for i in range(4):
                    act.wait_ge(res_ready[n], i + 1)
                    act.activation(sq[:, 2 * i:2 * i + 2, :], hT[:, 2 * i:2 * i + 2, :], ACT.Square
                                   ).then_inc(sq_ready[n], 1)

            def root(n, bank):
                act.wait_ge(ss_done[n], 1)
                act.activation(std[:, :], PS[:, bank, 0:SEQ], ACT.Sqrt, scale=1.0 / D, bias=eps[:, 0:1]
                               ).then_inc(std_ready[n], 1)

            load_small(act, SMALL_LOADS[1::2])
            act.wait_ge(eps_ready, 1)
            squares(0)
            root(0, 7)
            for c in range(KC):
                act.wait_ge(u_done, c + 1)
                if c >= 2:
                    act.wait_ge(glu_ready, c - 1)
                act.activation(sig[:, c % 2, :], PS[:, c, SEQ:2 * SEQ], ACT.Sigmoid).then_inc(sig_ready, 1)
                for j in range(POOL_TAPS if c < 2 else 0):
                    if j == 0:
                        act.wait_ge(vec_ready, 2)
                        act.wait_ge(glu_ready, c + 1)
                    elif j >= 3:
                        act.wait_ge(product_added, (POOL_TAPS - 1) * c + j - 2)
                    elif c and j:
                        act.wait_ge(product_added, (POOL_TAPS - 1) * c)
                    dst = conv_p[:, c, :] if j == 0 else products[:, j % 2, :]
                    act.activation(dst, glu[:, c, j:j + SEQ], ACT.Copy, scale=conv_w[:, c, j:j + 1]
                                   ).then_inc(product_ready, 1)
            act.wait_ge(pads, 2)
            for n, g in enumerate(POOL_ORDER):
                act.wait_ge(b_done, n + 1)
                act.activation(pool_in[:, g, PADP:], PS[:, 4 + g, 0:SEQ], ACT.Copy).then_inc(b_ready, 1)
            for n, g in enumerate(POOL_ORDER):
                act.wait_ge(pmap_done, n + 1)
                act.activation(mix[:, 4 + g, :], PS[:, *POOL_MAP[g]], ACT.Copy,
                               scale=col("pool_scale", g)).then_inc(pmix_ready, 1)
            def ff_split_high(g, q):
                act.wait_ge(ff_loaded[q], 16 * g + 16)
                if q == 2:
                    act.wait_ge(ff_down_done, HEAD + 4 * g)
                elif not (isinstance(g, int) and g == 0):
                    act.wait_ge((ff_h1_done, ff_h3_done)[q], 2 * g)
                act.activation(high[:, q, :], raw[:, FF_RAW[q], :], ACT.Copy).then_inc(ff_w_high, 1)

            for q in range(2):
                ff_split_high(0, q)
            for c in range(KC):
                act.wait_ge(cent_ready, c + 1)
                act.activation(sq[:, c, :], conv[:, c, :], ACT.Square).then_inc(lsq_ready, 1)
            act.wait_ge(var_done, 1)
            act.activation(std[:, :], PS[:, VAR, 0:SEQ], ACT.Sqrt, scale=1.0 / D_CONV, bias=eps[:, 0:1]
                           ).then_inc(lstd_ready, 1)
            for c in range(KC):
                act.wait_ge(ln_ready, c + 1)
                act.activation(mix[:, c, :], conv[:, c, :], ACT.Silu, bias=col("ln_b", c)).then_inc(cmix_ready, 1)
            squares(1)
            root(1, 7)

            def ff_group(g, last):
                ff_split_high(g, 2)
                for f in range(2):
                    act.wait_ge(ff_h1_done, 2 * g + f + 1)
                    act.wait_ge(ff_prod_ready, HEAD + 2 * g)
                    act.activation(ff_sg[:, f, :], PS[:, 4 + f, 0:SEQ], ACT.Silu).then_inc(ff_sg_ready, 1)
                if not last:
                    ff_split_high(g + 1, 0)
                for f in range(2):
                    act.wait_ge(ff_prod_ready, HEAD + 2 * g + f + 1)
                    act.activation(ff_high[:, f, :], ff_prod[:, f, :], ACT.Copy).then_inc(ff_high_ready, 1)
                if not last:
                    ff_split_high(g + 1, 1)

            act.wait_ge(wout_done, 4)
            for k in range(KD):
                act.wait_ge(hn_ready[1], k + 1)
                act.activation(hn_high[:, k, :], hn[:, k, :], ACT.Copy).then_inc(hn_high_ready, 1)
            with act.Fori(0, FFG - 1) as g:
                ff_group(g, False)
            ff_group(FFG - 1, True)

            squares(2)
            root(2, 7)

            for m in range(2):
                act.wait_ge(k_done, m + 1)
                for i in range(2):
                    r0 = HD * i
                    act.activation(kT[r0:r0 + HD, 2 * m + i, :], PS[r0:r0 + HD, m, 0:SEQ], ACT.Identity,
                                   bias=vec[r0:r0 + HD, VEC["b_qk"][0] + KD + m:VEC["b_qk"][0] + KD + m + 1]
                                   ).then_inc(k_half, 1)
            for b in range(NB):
                act.wait_ge(v_done, b + 1)
                act.activation(vN[:, b, :], PS[:, 2 + b, 0:NKV * HD], ACT.Copy).then_inc(v_ready, 1)

            def split_high(j, i, free=True):
                act.wait_ge(raw_loaded[raw_slot[i]], 16 * (UNITS // RAW) * j + 16 * (i // RAW + 1))
                if free:
                    act.wait_ge(unit_done, UNITS * j + i + 1)
                act.activation(high[:, i % SPLIT, :], raw[:, raw_slot[i], :], ACT.Copy).then_inc(high_ready, 1)

            for s in range(KD + 3):
                if s >= KD:
                    split_high(0, s - KD)
                if s < KD:
                    act.wait_ge(q_done, s + 1)
                    act.activation(qT[:, s, :], PS[:, 4 + s % 2, 0:SEQ], ACT.Identity, bias=col("b_qk", s)
                                   ).then_inc(q_ready, 1)
                if 0 <= s - 2 < KD:
                    m = s - 2
                    act.wait_ge(pT_done, 2 * m + 2)
                    if m >= 2:
                        act.wait_ge(o_done, m - 1)
                    act.activation(probsT[:, (2 * m + 1) % 4, :], PS[:, 1, 0:3 * P], ACT.Copy).then_inc(pT_act, 1)
                if 0 <= s - 3 < KD:
                    m = s - 3
                    act.wait_ge(o_done, m + 1)
                    act.activation(oT[:, m, :], PS[:, 2 + m % 2, 0:SEQ], ACT.Copy).then_inc(o_ready, 1)
                if 0 <= s - 1 < KD:
                    m = s - 1
                    act.wait_ge(neg_ready, m + 1)
                    for i in range(2):
                        h = 2 * m + i
                        for n, (a, z) in enumerate(((0, P), (P, 3 * P))):
                            c = 2 * h + n
                            act.activation(probs[:, h % 4, a:z], probs[:, h % 4, a:z], ACT.Exp,
                                           bias=negm[:, c:c + 1], accum_out=rsum[:, c:c + 1])
                        last = act.activation(esink[:, 2 * h:2 * h + 2], negm[:, 2 * h:2 * h + 2], ACT.Exp,
                                              bias=sinks[:, h:h + 1])
                    last.then_inc(e_ready, 1)
            act.wait_ge(pT_done, NH)
            squares(3)
            root(3, 0)
            for i in range(4):
                b, half = divmod(i, 2)
                act.wait_ge(acc_done, i + 1)
                act.activation(nat[:, b, half * 512:(half + 1) * 512], PS[:, 6 + i % 2, :], ACT.Copy).then_inc(acc_ready, 1)
            for i in range(4):
                act.wait_ge(tN_done, i + 1)
                if i == 0:
                    act.wait_ge(ss_done[3], 1)
                b, half = divmod(i, 2)
                act.activation(tN[:, b, half * 512:(half + 1) * 512], PS[:, 2 + i, :], ACT.Copy
                               ).then_inc(tN_ready, 1)
            act.wait_ge(top_ready, 1)
            act.activation(ratio, arg, ACT.Exp).then_inc(ratio_ready, 1)

            def take_tokens(j, halves=range(2)):
                for half in halves:
                    act.wait_ge(gathered, 2 * j + half + 1)
                    act.activation(x_high[:, 4 * half:4 * half + 4, :],
                                   PS[:, 2 + half, :].rearrange("p (k n) -> p k n", n=P), ACT.Copy
                                   ).then_inc(x_high_ready, 1)

            take_tokens(0)
            act.wait_ge(n_jobs_ready, 1)
            n_more = act.value_load(jobs_i[0:1, 2, 1:2], min_val=NE - 1, max_val=MAX_JOBS - 1)

            def job(j, last):
                for n in range(SPLIT, UNITS + SPLIT):
                    ahead, i = divmod(n, UNITS)
                    if not (last and ahead):
                        split_high(j + ahead, i)
                    if n - SPLIT in LAST_W1:
                        g = LAST_W1.index(n - SPLIT)
                        act.wait_ge(prod_ready, HEAD + GROUPS * j + g)
                        if g == 0:
                            act.wait_ge(back_done, HEAD + 4 * j)
                        act.activation(gate_h[:, :], PS[:, (0, 2)[g % 2], :], ACT.Silu).then_inc(gate_ready, 1)
                    if n in TAKE_H:
                        g = TAKE_H.index(n)
                        act.wait_ge(turned, GROUPS * j + g + 1)
                        if g == GROUPS - 1:
                            act.wait_ge(unit_done, UNITS * j + (SPLIT + UNITS - 2))
                        act.activation(h_high[:, :, :], PS[:, 6, :].rearrange("p (f n) -> p f n", n=P), ACT.Copy
                                       ).then_inc(h_high_ready, 1)
                    if n == UNITS and not last:
                        take_tokens(j + 1, [0])
                    if n == UNITS + 1:
                        for half in range(2):
                            act.wait_ge(unit_done, SPLIT + UNITS * j + UNITS)
                            act.activation(ys_high[:, half * 512:(half + 1) * 512], PS[:, 4 + half, :], ACT.Copy
                                           ).then_inc(ys_high_ready, 1)
                        if not last:
                            take_tokens(j + 1, [1])

            with act.Fori(0, n_more) as j:
                job(j, False)
            job(n_more, True)

            for b in range(NB):
                act.wait_ge(back_added, 4 * n_more + (HEAD + 2 * b + 2))
                act.activation(res[:, b, :], nat[:, b, :], ACT.Square, accum_out=ssq[:, b:b + 1]
                               ).then_inc(ssq_ready, 1)
                act.wait_ge(ssq_ready, b + 1)
                act.activation(frstd[:, b:b + 1], ssq[:, b:b + 1], ACT.Sqrt, scale=1.0 / D, bias=eps[:, 0:1]
                               ).then_inc(fstd_ready, 1)

        @block.vector
        def _(dve):
            def normed(n, gain, dst):
                dve.wait_ge(std_ready[n], 1)
                dve.reciprocal(rstd[:, :], std[:, :]).then_inc(rstd_ready[n], 1)
                dve.wait_ge(rstd_ready[n], 1)
                for k in range(KD):
                    dve.scalar_tensor_tensor(out=dst[:, k, :], in0=hT[:, k, :], scalar=col(gain, k), in1=rstd[:, :],
                                             op0=ALU.mult, op1=ALU.mult).then_inc(hn_ready[n], 1)

            for s in (ff_prod_ready, prod_ready, back_added):
                dve.sem_inc(s, HEAD)
            dve.memset(eps[:, :], RMS_EPS).then_inc(eps_ready, 1)
            for i in range(4):
                dve.wait_ge(xT_done, i + 1)
                dve.tensor_copy(hT[:, 2 * i:2 * i + 2, :], PS[:, i, :].rearrange("p (k n) -> p k n", n=SEQ)
                                ).then_inc(res_ready[0], 1)
            dve.wait_ge(vecT_done, 1)
            dve.tensor_copy(vec[:, :], PS[:, 4, 0:68]).then_inc(vec_ready, 1)
            dve.tensor_copy(conv_w[:, :, :], PS[:, 4, 128:256].rearrange("p (c n) -> p c n", n=32)[:, :, 0:CONV_K]
                            ).then_inc(vec_ready, 1)
            dve.wait_ge(consts, N_CONST)
            dve.reciprocal(inv_cnt[:, :, :], inv_cnt[:, :, :]).then_inc(vec_ready, 1)
            dve.wait_ge(vec_ready, 3)
            normed(0, "norm1", hn)

            steps = [0]

            def tap(ins, after=None):
                steps[0] += 1
                ins.then_inc(conv_step, 1)

            dve.wait_ge(pads, 2)
            for c in range(KC):
                dve.wait_ge(sig_ready, c + 1)
                dve.tensor_tensor(glu[:, c, PADC:], PS[:, c, 0:SEQ], sig[:, c % 2, :], ALU.mult
                                  ).then_inc(glu_ready, 1)
                dve.wait_ge(glu_ready, c + 1)
                if c:
                    dve.wait_ge(conv_ready, c)
                for j in range(POOL_TAPS if c < 2 else 0, CONV_K):
                    acc = conv[:, c, :] if j % 2 == 0 else conv_b2
                    src, w = glu[:, c, j:j + SEQ], conv_w[:, c, j:j + 1]
                    if j == (POOL_TAPS if c < 2 else 0):
                        tap(dve.tensor_scalar(acc, src, w, col("conv_b", c), ALU.mult, ALU.add))
                    elif j == (POOL_TAPS if c < 2 else 0) + 1:
                        tap(dve.tensor_scalar(acc, src, w, None, ALU.mult))
                    else:
                        dve.wait_ge(conv_step, steps[0] - 1)
                        tap(dve.scalar_tensor_tensor(out=acc, in0=src, scalar=w, in1=acc, op0=ALU.mult, op1=ALU.add))
                dve.wait_ge(conv_step, steps[0])
                if c < 2:
                    dve.wait_ge(product_added, (POOL_TAPS - 1) * (c + 1))
                    tap(dve.tensor_tensor(conv_b2, conv_b2, conv_p[:, c, :], ALU.add))
                    dve.wait_ge(conv_step, steps[0])
                dve.tensor_tensor(conv[:, c, :], conv[:, c, :], conv_b2, ALU.add).then_inc(conv_ready, 1)

            def ff_split_low(g, q):
                dve.wait_ge(ff_w_high, 3 * g + q + 1)
                dve.tensor_tensor(low[:, q, :], raw[:, FF_RAW[q], :], high[:, q, :].bitcast(F32), ALU.subtract
                                  ).then_inc(ff_w_low, 1)

            dve.wait_ge(mean_done, 1)
            for c in range(KC):
                dve.scalar_tensor_tensor(out=conv[:, c, :], in0=PS[:, MEAN, 0:SEQ], scalar=-1.0 / D_CONV,
                                         in1=conv[:, c, :], op0=ALU.mult, op1=ALU.add).then_inc(cent_ready, 1)
            dve.wait_ge(conv_ready, KC)
            ff_split_low(0, 0)
            dve.wait_ge(lstd_ready, 1)
            dve.reciprocal(rstd[:, :], std[:, :]).then_inc(lrstd_ready, 1)
            dve.wait_ge(lrstd_ready, 1)
            dve.wait_ge(lsq_ready, KC)
            for c in range(KC):
                dve.scalar_tensor_tensor(out=conv[:, c, :], in0=conv[:, c, :], scalar=col("ln_g", c),
                                         in1=rstd[:, :], op0=ALU.mult, op1=ALU.mult).then_inc(ln_ready, 1)
            dve.wait_ge(cent_ready, KC)
            for i in (MEAN, VAR):
                dve.memset(PS[:, i, :], 0.0).then_inc(ff_cleared, 1)

            def add_pair(n, i):
                dve.wait_ge(sq_ready[n], i + 1)
                dve.tensor_tensor(sq[:, 2 * i, :], sq[:, 2 * i, :], sq[:, 2 * i + 1, :], ALU.add
                                  ).then_inc(pair_ready[n], 1)

            def add_bank(i, bank):
                return dve.tensor_tensor(hT[:, 2 * i:2 * i + 2, :], PS[:, bank, :].rearrange("p (k n) -> p k n", n=SEQ),
                                         hT[:, 2 * i:2 * i + 2, :], ALU.add)

            for i in range(4):
                dve.wait_ge(wout_done, i + 1)
                add_bank(i, OUT_BANKS[i]).then_inc(res_ready[1], 1)
                add_pair(1, i)
            dve.wait_ge(res_ready[1], 4)
            for i in OUT_BANKS[0:2]:
                dve.memset(PS[:, i, :], 0.0).then_inc(ff_cleared, 1)
            normed(1, "norm2", hn)

            def ff_group(g, last):
                ff_split_low(g, 2)
                for f in range(2):
                    dve.wait_ge(ff_sg_ready, 2 * g + f + 1)
                    dve.wait_ge(ff_h3_done, 2 * g + f + 1)
                    dve.tensor_tensor(ff_prod[:, f, :], PS[:, 6 + f, 0:SEQ], ff_sg[:, f, :], ALU.mult
                                      ).then_inc(ff_prod_ready, 1)
                    dve.wait_ge(ff_high_ready, 2 * g + f + 1)
                    dve.tensor_tensor(ff_low[:, f, :], ff_prod[:, f, :], ff_high[:, f, :].bitcast(F32), ALU.subtract
                                      ).then_inc(ff_low_ready, 1)
                    if f == 0 and not last:
                        ff_split_low(g + 1, 0)
                if not last:
                    ff_split_low(g + 1, 1)

            for k in range(KD):
                dve.wait_ge(hn_high_ready, k + 1)
                dve.tensor_tensor(hn_low[:, k, :], hn[:, k, :], hn_high[:, k, :].bitcast(F32), ALU.subtract
                                  ).then_inc(hn_low_ready, 1)
            ff_split_low(0, 1)
            with dve.Fori(0, FFG - 1) as g:
                ff_group(g, False)
            ff_group(FFG - 1, True)
            for i in range(4):
                dve.wait_ge(ff_down_done, HEAD + 4 * (FFG - 1) + i + 1)
                add_bank(i, i).then_inc(res_ready[2], 1)
            dve.wait_ge(res_ready[2], 4)
            normed(2, "onorm1", hn)

            for j in range(NKV):
                dve.wait_ge(k_half, j + 1)
                a, z = (0, HD) if j % 2 == 0 else (HD, 2 * HD)
                dve.tensor_copy(kT[HD - a:2 * HD - a, j, :], kT[a:z, j, :]).then_inc(k_ready, 1)

            dve.wait_ge(const_step, MASK_STEPS)
            dve.wait_ge(small_loaded, 16 * N_SMALL)
            dsteps = [0]

            def link(ins):
                dsteps[0] += 1
                ins.then_inc(den_step, 1)
                dve.wait_ge(den_step, dsteps[0])

            for s in range(1, KD + 3):
                if 0 <= s - 2 < KD:
                    m = s - 2
                    c = slice(4 * m, 4 * m + 4)
                    dve.wait_ge(e_ready, m + 1)
                    link(dve.tensor_tensor(den[:, c], rsum[:, c], esink[:, c], ALU.add))
                    link(dve.reciprocal(rden[:, c], den[:, c]))
                    for i in range(2):
                        h = 2 * m + i
                        for n, (a, z) in enumerate(((0, P), (P, 3 * P))):
                            last = dve.tensor_scalar(probs[:, h % 4, a:z], probs[:, h % 4, a:z],
                                                     rden[:, 2 * h + n:2 * h + n + 1], None, ALU.mult)
                    last.then_inc(p_ready, 1)
                if 0 <= s - 1 < KD:
                    m = s - 1
                    for i in range(2):
                        h = 2 * m + i
                        dve.wait_ge(s_done, h + 1)
                        if h >= 4:
                            dve.wait_ge(pT_done, h - 3)
                        elif h == 0:
                            dve.wait_ge(ss_done[2], 1)
                        for n, (a, z) in enumerate(((0, P), (P, 3 * P))):
                            last = dve.tensor_tensor_reduce(
                                out=probs[:, h % 4, a:z], in0=PS[:, 6 + i, a:z], in1=mask[:, a:z], scale=SCALE,
                                scalar=sinks[:, h:h + 1], op0=ALU.add, op1=ALU.max,
                                accum_out=mx[:, 2 * h + n:2 * h + n + 1])
                        last.then_inc(s_masked, 1)
                    dve.wait_ge(s_masked, 2 * m + 2)
                    dve.tensor_scalar(negm[:, 4 * m:4 * m + 4], mx[:, 4 * m:4 * m + 4], -1.0, None, ALU.mult
                                      ).then_inc(neg_ready, 1)
                if 0 <= s - 2 < KD:
                    m = s - 2
                    dve.wait_ge(pT_done, 2 * m + 1)
                    if m >= 2:
                        dve.wait_ge(o_done, m - 1)
                    dve.tensor_copy(probsT[:, (2 * m) % 4, :], PS[:, 0, 0:3 * P]).then_inc(pT_dve, 1)

            def split_low(j, i):
                dve.wait_ge(high_ready, UNITS * j + i + 1)
                dve.tensor_tensor(low[:, i % SPLIT, :], raw[:, raw_slot[i], :], high[:, i % SPLIT, :].bitcast(F32),
                                  ALU.subtract).then_inc(low_ready, 1)

            dve.wait_ge(s_done, NH)
            split_low(0, 0)
            dve.wait_ge(o_done, KD)
            split_low(0, 1)
            for i in range(4):
                dve.wait_ge(wo_done, i + 1)
                for kk in range(2):
                    k = 2 * i + kk
                    last = dve.scalar_tensor_tensor(out=hT[:, k, :], in0=PS[:, 4 + i, kk * SEQ:(kk + 1) * SEQ],
                                                    scalar=col("b_o", k), in1=hT[:, k, :], op0=ALU.add, op1=ALU.add)
                last.then_inc(res_ready[3], 1)
                add_pair(3, i)
            dve.wait_ge(res_ready[3], 4)
            split_low(0, 2)
            normed(3, "onorm2", hn)

            rsteps = [0]

            def then(ins):
                rsteps[0] += 1
                ins.then_inc(route, 1)
                dve.wait_ge(route, rsteps[0])

            def wide(ap):
                return ap.unsqueeze(2).broadcast_to([P, NB, NE])

            def choose(values, top, which):
                then(dve.tensor_reduce(top, values, X, ALU.max))
                then(dve.tensor_tensor(less, values, wide(top), ALU.is_lt))
                then(dve.scalar_tensor_tensor(out=place, in0=less, scalar=float(2 * NE), in1=iota_e,
                                              op0=ALU.mult, op1=ALU.add))
                then(dve.tensor_reduce(arg, place, X, ALU.min))
                then(dve.tensor_tensor(which, iota_e, wide(arg), ALU.is_equal))

            dve.wait_ge(logitT_done, 1)
            dve.tensor_copy(logitsT, PS[0:NE, 1, 128:128 + SEQ]).then_inc(logitT_ready, 1)
            dve.wait_ge(logit_done, 1)
            then(dve.tensor_copy(logits, PS[:, 1, 0:NB * NE].rearrange("p (b e) -> p b e", b=NB)))
            choose(logits, top1, first)
            then(dve.scalar_tensor_tensor(out=logits, in0=first, scalar=-3e38, in1=logits, op0=ALU.mult, op1=ALU.add))
            choose(logits, top2, second)
            dve.tensor_tensor(chosen, first, second, ALU.add).then_inc(chosen_ready, 1)
            dve.tensor_tensor(arg, top2, top1, ALU.subtract).then_inc(top_ready, 1)
            dve.wait_ge(place_done, 1)
            dve.wait_ge(chosen_ready, 1)
            then(dve.scalar_tensor_tensor(out=slots, in0=PS[:, 1, 32:32 + NB * NE].rearrange("p (b e) -> p b e", b=NB),
                                          scalar=1.0, in1=chosen, op0=ALU.add, op1=ALU.mult))
            then(dve.tensor_scalar(slots, slots, -1.0, None, ALU.add))
            count, need, run, run2 = je[:, 0, 0:NE], je[:, 1, 0:NE], je[:, 2, 0:NE], je[:, 3, 0:NE]
            total = je[:, 0, NE:NE + 1]
            owner, begin, offs, left = je[:, 4, 0:NJ], je[:, 5, 0:NJ], je[:, 6, 0:NJ], je[:, 7, 0:NJ]
            then(dve.tensor_copy(count, PS[:, 1, 64:64 + NE]))
            then(dve.tensor_scalar(need, count, float(JOB), 1.0, ALU.is_gt, ALU.add))
            then(dve.tensor_reduce(total, need, X, ALU.add))
            then(dve.tensor_copy(jobs_i[0:1, 2, 0:1], total[0:1]))
            dve.tensor_scalar(jobs_i[0:1, 2, 1:2], total[0:1], -1.0, None, ALU.add).then_inc(n_jobs_ready, 1)

            def select(j, e, offset=True):
                for b in range(NB):
                    last = dve.tensor_scalar(sel[:, b, :], iota_f[:, :], offs[:, bass.ds(j, 1)] if offset else 0.0,
                                             slots[:, b, bass.ds(e, 1)], ALU.add, ALU.is_equal)
                last.then_inc(sel_ready, 1)

            dve.wait_ge(acc_ready, 4)
            select(0, 0, offset=False)

            dve.wait_ge(ratio_ready, 1)
            then(dve.tensor_scalar(share2, ratio, 1.0, None, ALU.add))
            then(dve.reciprocal(share1, share2))
            then(dve.tensor_tensor(share2, ratio, share1, ALU.mult))
            then(dve.tensor_tensor(first, first, wide(share1), ALU.mult))
            then(dve.tensor_tensor(second, second, wide(share2), ALU.mult))
            then(dve.tensor_tensor(gates, first, second, ALU.add))

            src, dst = need, run
            for s in (1, 2, 4):
                then(dve.tensor_copy(dst[:, 0:s], src[:, 0:s]))
                then(dve.tensor_tensor(dst[:, s:], src[:, s:], src[:, 0:NE - s], ALU.add))
                src, dst = dst, (run2 if dst is run else run)
            then(dve.tensor_tensor(dst, src, need, ALU.subtract))
            start = dst
            by_job = [P, NJ, NE]

            def over_jobs(ap):
                return ap.unsqueeze(1).broadcast_to(by_job)

            def over_experts(ap):
                return ap.unsqueeze(2).broadcast_to(by_job)

            number = iota_f[:, 0:NJ]
            then(dve.tensor_tensor(jt[:, 0], over_experts(number), over_jobs(start), ALU.is_ge))
            then(dve.tensor_reduce(owner, jt[:, 0], X, ALU.add))
            then(dve.tensor_tensor(jt[:, 1], jt[:, 0], over_jobs(start), ALU.mult))
            then(dve.tensor_reduce(begin, jt[:, 1], X, ALU.max))

            def take_sel(j):
                dve.wait_ge(selT_done, j + 1)
                dve.tensor_copy(selT[:, :], PS[:, 2, 0:NB * P]).then_inc(selT_ready, 1)

            def take_tokens(j, halves=range(2)):
                for half in halves:
                    dve.wait_ge(x_high_ready, 2 * j + half + 1)
                    dve.tensor_tensor(x_low[:, 4 * half:4 * half + 4, :],
                                      PS[:, 2 + half, :].rearrange("p (k n) -> p k n", n=P),
                                      x_high[:, 4 * half:4 * half + 4, :].bitcast(F32), ALU.subtract
                                      ).then_inc(x_low_ready, 1)

            take_tokens(0)
            take_sel(0)
            then(dve.tensor_scalar(owner, owner, -1.0, None, ALU.add))
            then(dve.tensor_tensor(jt[:, 2], over_experts(owner), over_jobs(iota_f[:, 0:NE]), ALU.is_equal))
            then(dve.tensor_tensor(jt[:, 3], jt[:, 2], over_jobs(count), ALU.mult))
            then(dve.tensor_reduce(left, jt[:, 3], X, ALU.add))
            then(dve.tensor_tensor(offs, number, begin, ALU.subtract))
            then(dve.tensor_scalar(offs, offs, float(JOB), None, ALU.mult))
            then(dve.tensor_tensor(left, left, offs, ALU.subtract))
            then(dve.tensor_copy(jobs_i[0:1, 0, :], owner[0:1]))
            dve.tensor_copy(jobs_i[0:1, 1, :], left[0:1]).then_inc(jobs_ready, 1)
            dve.wait_ge(jobs_ready, 1)

            def add_back(j, e, banks):
                for k in banks:
                    b, half = divmod(k, 2)
                    dve.wait_ge(back_done, HEAD + 4 * j + k + 1)
                    dst = nat[:, b, half * 512:(half + 1) * 512]
                    dve.scalar_tensor_tensor(out=dst, in0=PS[:, (6, 7, 4, 5)[k], :], scalar=gates[:, b, bass.ds(e, 1)],
                                             in1=dst, op0=ALU.mult, op1=ALU.add).then_inc(back_added, 1)

            n_more = dve.value_load(jobs_i[0:1, 2, 1:2], min_val=NE - 1, max_val=MAX_JOBS - 1)

            def job(j, last):
                e = dve.value_load(jobs_i[0:1, 0, bass.ds(j, 1)], min_val=0, max_val=NE - 1)
                if not last:
                    e_next = dve.value_load(jobs_i[0:1, 0, bass.ds(j + 1, 1)], min_val=0, max_val=NE - 1)
                    select(j + 1, e_next)

                def take_hidden(n):
                    g = TAKE_H.index(n)
                    dve.wait_ge(h_high_ready, GROUPS * j + g + 1)
                    dve.tensor_tensor(h_low[:, :, :], PS[:, 6, :].rearrange("p (f n) -> p f n", n=P),
                                      h_high[:, :, :].bitcast(F32), ALU.subtract).then_inc(h_low_ready, 1)

                for n in range(SPLIT, UNITS + SPLIT):
                    ahead, i = divmod(n, UNITS)
                    if n == TAKE_H[-1]:
                        take_hidden(n)
                    if not (last and ahead):
                        split_low(j + ahead, i)
                    if n - 2 in LAST_UP:
                        g = LAST_UP.index(n - 2)
                        dve.wait_ge(gate_ready, GROUPS * j + g + 1)
                        dve.wait_ge(unit_done, SPLIT + UNITS * j + LAST_UP[g] + 1)
                        dve.tensor_tensor(prod_h[:, :], PS[:, (1, 3)[g % 2], :], gate_h[:, :], ALU.mult
                                          ).then_inc(prod_ready, 1)
                    if n in TAKE_H[:-1]:
                        take_hidden(n)
                    if n == UNITS:
                        if not last:
                            take_tokens(j + 1, [0])
                        for half in range(2):
                            dve.wait_ge(ys_high_ready, 2 * j + half + 1)
                            cols = slice(half * 512, (half + 1) * 512)
                            dve.tensor_tensor(ys_low[:, cols], PS[:, 4 + half, :], ys_high[:, cols].bitcast(F32),
                                              ALU.subtract).then_inc(ys_low_ready, 1)
                    if n == UNITS + 1:
                        if not last:
                            take_tokens(j + 1, [1])
                        add_back(j, e, range(2))
                    if n == UNITS + 2:
                        add_back(j, e, range(2, 4))
                        if not last:
                            take_sel(j + 1)

            with dve.Fori(0, n_more) as j:
                job(j, False)
            job(n_more, True)

            for b in range(NB):
                dve.wait_ge(fstd_ready, b + 1)
                dve.reciprocal(frstd[:, b:b + 1], frstd[:, b:b + 1]).then_inc(frstd_ready, 1)
                dve.wait_ge(frstd_ready, b + 1)
                dve.wait_ge(fnorm_loaded, 16)
                for half in range(2):
                    cols = slice(half * D // 2, (half + 1) * D // 2)
                    dve.scalar_tensor_tensor(out=res[:, b, cols], in0=nat[:, b, cols], scalar=frstd[:, b:b + 1],
                                             in1=fnorm[:, cols], op0=ALU.mult, op1=ALU.mult
                                             ).then_inc(final_ready, 1)


_INS = ["x", "e_norm1", "e_w_in", "e_conv_w", "e_conv_b", "e_ln_g", "e_ln_b", "e_pool_w", "e_pool_scale",
        "e_w_out", "e_norm2", "e_ff_w1", "e_ff_w3", "e_ff_w2", "o_norm1", "o_w_qkv", "o_b_qkv", "o_sinks",
        "o_w_o", "o_b_o", "o_norm2", "o_router", "o_exp_w1", "o_exp_w3", "o_exp_w2", "final_norm"]


def kernel(**inputs):
    import numpy as _np
    import concourse.bacc as _bacc
    from concourse import mybir as _mybir
    from concourse.bass_utils import run_bass_kernel_spmd as _run

    nc = _bacc.Bacc("TRN2", target_bir_lowering=False, num_devices=1)
    arrays, args = {}, []
    for name in _INS:
        a = _np.ascontiguousarray(inputs[name])
        arrays[f"in_{name}_dram"] = a
        args.append(nc.dram_tensor(f"in_{name}_dram", a.shape, _mybir.dt.from_np(a.dtype), kind="ExternalInput").ap())
    shape = tuple(inputs["x"].shape)
    args.append(nc.dram_tensor("out_dram", shape, _mybir.dt.float32, kind="ExternalOutput").ap())
    hybrid_trunk(nc, *args)
    r = _run(nc, [arrays], core_ids=[0])
    return r.results[0]["out_dram"]
```
